# Optimizing a Trainium2 kernel written in Bass

```python
import jax, jax.numpy as jnp
from jax import lax
import numpy as np

D_MODEL = 1024
BATCH = 1
SEQ = 1024
DEPTH = 1

D_MIX = D_MODEL
HEAD_DIM = 64
N_ATT_HEADS = 8
D_ATT = N_ATT_HEADS * HEAD_DIM
N_GM_GROUPS = 8
GM_GROUP_DIM = 64
D_GM = N_GM_GROUPS * GM_GROUP_DIM
BLOCK = 128
CHUNK = 128
D_IN = 3 * D_ATT + N_ATT_HEADS + 2 * D_GM
D_FF = ((8 * D_MODEL // 3 + 255) // 256) * 256
PLE_DIM = 256
EPS = 1e-6
NEG_INF = -1e30

kernel_name = "hybrid_fox_gmlp_sandwich_ple"

def rmsnorm(x, gain=None):
    xf = x.astype(jnp.float32)
    y = xf * lax.rsqrt(jnp.mean(xf * xf, axis=-1, keepdims=True) + EPS)
    if gain is not None:
        y = y * gain.astype(jnp.float32)
    return y.astype(x.dtype)

def fox_attention(q, k, v, log_f):
    S = q.shape[1]
    dh = q.shape[-1]
    scale = dh ** -0.5
    c = jnp.cumsum(log_f.astype(jnp.float32), axis=1).transpose(0, 2, 1)
    q_idx = jnp.arange(BLOCK)
    outs = []
    for i in range(S // BLOCK):
        lo, hi = i * BLOCK, (i + 1) * BLOCK
        s = jnp.einsum('bqhd,bkhd->bhqk', q[:, lo:hi], k[:, :hi],
                       preferred_element_type=jnp.float32) * scale
        s = s + c[:, :, lo:hi, None] - c[:, :, None, :hi]
        causal = (lo + q_idx)[:, None] >= jnp.arange(hi)[None, :]
        s = jnp.where(causal, s, NEG_INF)
        w = jax.nn.softmax(s, axis=-1).astype(v.dtype)
        outs.append(jnp.einsum('bhqk,bkhd->bqhd', w, v[:, :hi]))
    return jnp.concatenate(outs, axis=1)

def chunked_spatial_gating(g, w_s, b_s, v_gain):
    B, S, _ = g.shape
    u, vv = jnp.split(jax.nn.gelu(g), 2, axis=-1)
    shp = (B, S // CHUNK, CHUNK, N_GM_GROUPS, GM_GROUP_DIM)
    vf = vv.reshape(shp).astype(jnp.float32)
    mu = jnp.mean(vf, axis=-1, keepdims=True)
    var = jnp.mean(jnp.square(vf - mu), axis=-1, keepdims=True)
    vn = ((vf - mu) * lax.rsqrt(var + EPS) * v_gain.reshape(N_GM_GROUPS, GM_GROUP_DIM).astype(jnp.float32)).astype(g.dtype)
    tril = jnp.tril(jnp.ones((CHUNK, CHUNK), dtype=w_s.dtype))
    w = w_s * tril[None]
    mixed = jnp.einsum('gts,bnsgd->bntgd', w, vn) + b_s.T[:, :, None]
    return (u.reshape(shp) * mixed).reshape(B, S, D_GM)

def setup_inputs(seed: int = 0) -> dict:
    key = jax.random.key(seed)
    ks = jax.random.split(key, 20)
    L = DEPTH
    f32 = jnp.float32
    def nrm(k, shape, scale):
        return jax.random.normal(k, shape, f32) * scale
    def gain(k, shape):
        return 1.0 + 0.05 * jax.random.normal(k, shape, f32)
    return {
        "x": jax.random.normal(ks[0], (BATCH, SEQ, D_MODEL), f32),
        "p": jax.random.normal(ks[1], (DEPTH, BATCH, SEQ, PLE_DIM), f32),
        "mix_pre_norm": gain(ks[2], (L, D_MODEL)),
        "mix_post_norm": gain(ks[3], (L, D_MODEL)),
        "w_in": nrm(ks[4], (L, D_MODEL, D_IN), D_MODEL ** -0.5),
        "b_forget": jax.random.uniform(ks[5], (L, N_ATT_HEADS), f32, 2.0, 6.0),
        "gm_v_norm": gain(ks[6], (L, D_GM)),
        "gm_w_s": nrm(ks[7], (L, N_GM_GROUPS, CHUNK, CHUNK), 0.5 * CHUNK ** -0.5),
        "gm_b_s": 1.0 + 0.05 * jax.random.normal(ks[8], (L, N_GM_GROUPS, CHUNK), f32),
        "mix_out_norm": gain(ks[9], (L, D_MIX)),
        "w_out": nrm(ks[10], (L, D_MIX, D_MODEL), D_MIX ** -0.5),
        "ffn_pre_norm": gain(ks[11], (L, D_MODEL)),
        "ffn_post_norm": gain(ks[12], (L, D_MODEL)),
        "w_ffn_in": nrm(ks[13], (L, D_MODEL, 2 * D_FF), D_MODEL ** -0.5),
        "w_ffn_out": nrm(ks[14], (L, D_FF, D_MODEL), D_FF ** -0.5),
        "w_ple": nrm(ks[15], (L, PLE_DIM, D_MODEL), PLE_DIM ** -0.5),
        "ple_norm": gain(ks[16], (L, D_MODEL)),
        "w_ple_gate": nrm(ks[17], (L, D_MODEL, D_MODEL), D_MODEL ** -0.5),
    }

def reference(x, p, mix_pre_norm, mix_post_norm, w_in, b_forget, gm_v_norm, gm_w_s,
              gm_b_s, mix_out_norm, w_out, ffn_pre_norm, ffn_post_norm, w_ffn_in,
              w_ffn_out, w_ple, ple_norm, w_ple_gate):
    B, S, _ = x.shape
    h = x
    for i in range(DEPTH):
        hn = rmsnorm(h, mix_pre_norm[i])
        z = hn @ w_in[i]
        q, k, v, f_logit, g = jnp.split(
            z, [D_ATT, 2 * D_ATT, 3 * D_ATT, 3 * D_ATT + N_ATT_HEADS], axis=-1)
        q = q.reshape(B, S, N_ATT_HEADS, HEAD_DIM)
        k = k.reshape(B, S, N_ATT_HEADS, HEAD_DIM)
        v = v.reshape(B, S, N_ATT_HEADS, HEAD_DIM)
        log_f = jax.nn.log_sigmoid(f_logit.astype(jnp.float32) + b_forget[i].astype(jnp.float32))
        att = fox_attention(q, k, v, log_f).reshape(B, S, D_ATT)
        gm = chunked_spatial_gating(g, gm_w_s[i], gm_b_s[i], gm_v_norm[i])
        g_att, g_gm = jnp.split(mix_out_norm[i], [D_ATT])
        mixed = jnp.concatenate([rmsnorm(att, g_att), rmsnorm(gm, g_gm)], axis=-1)
        h = h + rmsnorm(mixed @ w_out[i], mix_post_norm[i])
        hn = rmsnorm(h, ffn_pre_norm[i])
        a, b = jnp.split(hn @ w_ffn_in[i], 2, axis=-1)
        h = h + rmsnorm((jax.nn.silu(a) * b) @ w_ffn_out[i], ffn_post_norm[i])
        e = rmsnorm(p[i] @ w_ple[i], ple_norm[i])
        gate = jax.nn.sigmoid(rmsnorm(h) @ w_ple_gate[i])
        h = h + gate * e
    return h


_drawn_inputs = setup_inputs


def setup_inputs(seed=0):
    import zlib

    import numpy as np

    out = dict(_drawn_inputs(seed))
    spreads = {}
    factors = {'gm_v_norm': 19.009, 'ple_norm': 3.853, 'gm_b_s': 5.955, 'ffn_post_norm': 2.842}
    for name, (base, spread) in spreads.items():
        noise = np.random.default_rng([zlib.crc32(name.encode()), seed]).standard_normal(out[name].shape)
        drawn = base * np.exp(spread * noise) if base else spread * noise
        out[name] = __import__('jax').numpy.asarray(drawn.astype(out[name].dtype))
    for name, factor in factors.items():
        out[name] = (out[name] * factor).astype(out[name].dtype)
    return out
```

```python
import concourse.bass as bass
import numpy as np
from concourse import mybir

TOKENS, D_MODEL = 1024, 1024
HEADS, HEAD_DIM = 8, 64
D_ATT = HEADS * HEAD_DIM
GROUPS, GROUP_DIM, CHUNK = 8, 64, 128
D_GM = GROUPS * GROUP_DIM
D_FF = ((8 * D_MODEL // 3 + 255) // 256) * 256
PLE_DIM = 256
EPS = 1e-6

P = 128
TT = TOKENS // P
KT = D_MODEL // P
FT = D_FF // P
PAIRS = HEADS // 2
BANK = 512
UNIT = 1024
NT_COLS = D_MODEL // P

U_GATING, U_QK, U_MIX = 0, 12, 20
U_FFN = U_MIX + 8
U_GATE = U_FFN + 3 * FT
U_PLE = U_GATE + 8
UNITS = U_PLE + 2
RAW_SLOTS, WEIGHT_SLOTS = 2, 4


class Steps:

    def __init__(self, engine, semaphore):
        self.engine, self.semaphore, self.done, self.turn = engine, semaphore, 0, 0

    def __call__(self, instruction):
        instruction.then_inc(self.semaphore, 1)
        self.done += 1
        self.engine.wait_ge(self.semaphore, self.turn + self.done)

    def loop(self, i, per):
        self.start, self.per, self.turn = self.done, per, i * per

    def end_loop(self, turns):
        assert self.done - self.start == self.per
        self.done, self.turn = self.start + turns * self.per, 0


def build_trunk(nc, x, weights, w_forget, b_forget, p_t, ws_t, b_s, gains, gm_gain, c_scratch, out):
    fp32, fp32r, bf16 = mybir.dt.float32, mybir.dt.float32r, mybir.dt.bfloat16
    ALU, ACT, AX = mybir.AluOpType, mybir.ActivationFunctionType, mybir.AxisListType

    KB = 1024
    base = (nc.sbuf_base + 63) // 64 * 64
    at = {"ring": base, "raw": base + 32 * KB, "gain": base + 40 * KB, "hn": base + 48 * KB,
          "f": base + 112 * KB, "small": base + 204 * KB}

    def place(name, shape, dtype, region, kb=0.0):
        return nc.alloc_sbuf_tensor_at(name, [P, *shape], dtype, offset=at[region] + int(kb * KB))

    w_raw = place("w_raw", [RAW_SLOTS, UNIT], fp32, "raw")
    w_split = [place(f"w_split{s}", [2, UNIT], fp32r, "ring", 8 * s) for s in range(WEIGHT_SLOTS)]
    gain = place("gain", [2, D_MODEL], fp32, "gain")
    hn = place("hn", [2, KT, TOKENS], fp32r, "hn")

    x_tiles = place("x_tiles", [TT, D_MODEL], fp32, "f", 0)
    xn_first = place("xn_first", [4, D_MODEL], fp32, "f", 48)
    gv = place("gv", [TT, D_GM], fp32, "f", 0)
    gu = place("gu", [TT, D_GM], fp32, "f", 16)
    v_raw = place("v_raw", [TT, D_ATT], fp32, "f", 32)
    vn = place("vn", [2, TT, D_GM], fp32r, "f", 48)
    qk_raw = place("qk_raw", [PAIRS, 2, TOKENS], fp32, "f", 48)
    squares = place("squares", [2, D_GM], fp32, "f", 48)
    ws_split = place("ws_split", [2, GROUPS, CHUNK], fp32r, "f", 80)
    ws_raw = place("ws_raw", [GROUPS, CHUNK], fp32, "f", 88)

    p_turned = [place(f"p_turned{s}", [2, TT, 256], fp32r, "hn", 16 * s) for s in range(2)]
    q2 = [place(f"q2_{a}", [TOKENS], fp32r, "hn", 32 + 4 * a) for a in range(2)]
    k2 = [place(f"k2_{a}", [2, TOKENS], fp32r, "hn", 40 + 8 * a) for a in range(2)]
    v2 = place("v2", [TT, 2, 2, HEAD_DIM], fp32r, "hn", 56)
    probs = place("probs", [4, TOKENS], fp32, "f", 0)
    forget_bias = place("forget_bias", [2, TOKENS], fp32, "f", 80)
    out_t = place("out_t", [256], fp32, "f", 88)
    forget = place("forget", [4, TOKENS], fp32, "f", 0)
    wf_raw = place("wf_raw", [KT, HEADS], fp32, "f", 89)
    wf_split = place("wf_split", [2, KT, HEADS], fp32r, "f", 89.5)

    xn_mix = place("xn_mix", [4, D_MODEL], fp32, "f", 0)
    y = place("y", [TT, D_MODEL], fp32, "f", 0)
    h = place("h", [TT, D_MODEL], fp32, "f", 32)
    xn_late = place("xn_late", [4, D_MODEL], fp32, "f", 64)
    hid = [place(f"hid{s}", [2, TOKENS], fp32r, "f", 64 + 8 * s) for s in range(2)]
    silu_a = place("silu_a", [2, BANK], fp32, "f", 80)
    hid_raw = place("hid_raw", [2, BANK], fp32, "f", 84)
    pt_raw = place("pt_raw", [2, TOKENS], fp32, "f", 80)
    pt_split = place("pt_split", [2, 2, TOKENS], fp32r, "f", 64)
    e_tile = place("e_tile", [2, D_MODEL], fp32, "f", 80)

    ident = place("ident", [P], fp32, "small", 0)
    ident_bf = place("ident_bf", [P], bf16, "small", 0.5)
    causal_bf = place("causal_bf", [P], bf16, "small", 0.75)
    fold = place("fold", [HEAD_DIM], fp32, "small", 1)
    bs_col = place("bs_col", [GROUPS], fp32, "small", 1.25)
    bf_col = place("bf_col", [1], fp32, "small", 1.3125)
    row_sum = place("row_sum", [2 * TT], fp32, "small", 1.375)
    row_inv = place("row_inv", [2 * TT], fp32, "small", 1.5)
    neg_max = place("neg_max", [2 * TT], fp32, "small", 1.625)
    g_sum = place("g_sum", [TT * GROUPS], fp32, "small", 1.75)
    g_var = place("g_var", [TT * GROUPS], fp32, "small", 2)
    g_inv = place("g_inv", [TT * GROUPS], fp32, "small", 2.25)
    stat = place("stat", [7, 3, 2, TT], fp32, "small", 2.5)
    eps = place("eps", [1], fp32, "small", 3.8125)
    ps = nc.alloc_psum_tensor("ps", [P, 8, BANK], fp32)

    def sem(name):
        return nc.alloc_semaphore(name)

    raw_in = [sem(f"raw_in{s}") for s in range(RAW_SLOTS)]
    high_made, w_ready, w_used = sem("high_made"), sem("w_ready"), sem("w_used")
    x_in = [sem(f"x_in{t}") for t in range(TT)]
    h_in = [sem(f"h_in{t}") for t in range(TT)]
    const_in, ws_in, pt_in, gain_in = sem("const_in"), sem("ws_in"), sem("pt_in"), sem("gain_in")
    pool_passed, dve_passed = sem("pool_passed"), sem("dve_passed")
    consts_made, wf_in, wf_ready = sem("consts_made"), sem("wf_in"), sem("wf_ready")
    ws_masked, ws_high, ws_ready = sem("ws_masked"), sem("ws_high"), sem("ws_ready")
    dve_step, act_step = sem("dve_step"), sem("act_step")
    norms = {n: {k: sem(f"norm_{n}_{k}") for k in ("squared", "rooted", "scaled", "turned", "high", "split")}
             for n in ("pre", "mix", "ffn", "gate")}
    chunk_done, chunk_out = sem("chunk_done"), sem("chunk_out")
    var_ready, var_rooted, vn_scaled, vn_high, vn_ready = (
        sem("var_ready"), sem("var_rooted"), sem("vn_scaled"), sem("vn_high"), sem("vn_ready"))
    spatial_done, spatial_out = sem("spatial_done"), sem("spatial_out")
    qk_done, qk_out, f_done, f_logit, f_exp, f_ln, c_ready, c_out = (
        sem("qk_done"), sem("qk_out"), sem("f_done"), sem("f_logit"), sem("f_exp"), sem("f_ln"),
        sem("c_ready"), sem("c_out"))
    bias_in, bias_free = sem("bias_in"), sem("bias_free")
    heads_high, heads_ready = sem("heads_high"), sem("heads_ready")
    scores_done, scored, exped, p_moved, p_high, p_split = (
        sem("scores_done"), sem("scored"), sem("exped"), sem("p_moved"), sem("p_high"), sem("p_split"))
    pv_done, out_t_made, folded, attended = sem("pv_done"), sem("out_t_made"), sem("folded"), sem("attended")
    mix_done, mix_out = sem("mix_done"), sem("mix_out")
    post_squared, post_rooted, h_ready = sem("post_squared"), sem("post_rooted"), sem("h_ready")
    a_done, a_out, b_done, hid_made, hid_high, hid_ready, out_done, out_added = (
        sem("a_done"), sem("a_out"), sem("b_done"), sem("hid_made"), sem("hid_high"),
        sem("hid_ready"), sem("out_done"), sem("out_added"))
    ffn_squared, ffn_rooted, h2_ready = sem("ffn_squared"), sem("ffn_rooted"), sem("h2_ready")
    gate_done, gate_out, pt_high, pt_ready = sem("gate_done"), sem("gate_out"), sem("pt_high"), sem("pt_ready")
    ple_done, e_scaled, e_squared, e_rooted, row_ready, stored = (
        sem("ple_done"), sem("e_scaled"), sem("e_squared"), sem("e_rooted"), sem("row_ready"),
        sem("stored"))

    G_PRE, G_MIX, G_POST, G_FFN, G_FFN_POST, G_PLE = range(6)
    SQRT_ALL, SQRT_HALF = 1.0 / D_MODEL, 1.0 / D_ATT

    TILES = [(a, q) for a in range(2) for q in range(TT)]
    PARTS = [q // 4 + 1 for _, q in TILES]
    PART_AT = [sum(PARTS[:j]) for j in range(len(TILES) + 1)]
    BLOCKS = len(TILES) // 2
    DEPTH = 5

    def chunk_full(engine, done, chunk, first_unit, t):
        if t < TT - 1:
            engine.wait_ge(done, (TT - 1) * chunk + t + 1)
        else:
            engine.wait_ge(w_used, first_unit + 4 * chunk + 4)

    def tile_full(engine, done, tiles, unit, half):
        if half == 0:
            engine.wait_ge(done, tiles + 1)
        else:
            engine.wait_ge(w_used, unit + 1)

    block = nc.Block()
    with block:

        @block.sync
        def _(sp):
            for s in range(RAW_SLOTS):
                sp.dma_start(w_raw[:, s, :], weights[s]).then_inc(raw_in[s], 16)
            with sp.Fori(1, UNITS // RAW_SLOTS) as i:
                for s in range(RAW_SLOTS):
                    sp.wait_ge(w_ready, RAW_SLOTS * i + (s + 1 - RAW_SLOTS))
                    sp.dma_start(w_raw[:, s, :], weights[bass.ds(RAW_SLOTS * i + s, 1)][0]
                                 ).then_inc(raw_in[s], 16)
            for t in range(TT):
                sp.wait_ge(row_ready, t + 1)
                sp.dma_start(out[t * P:(t + 1) * P, :], h[:, t, :]).then_inc(stored, 16)
            sp.wait_ge(stored, 16 * TT)

        @block.gpsimd
        def _(pool):
            pool.memset(ident[:, :], 0.0).then_inc(consts_made, 1)
            pool.memset(ident_bf[:, :], 0.0).then_inc(consts_made, 1)
            pool.memset(causal_bf[:, :], 0.0).then_inc(consts_made, 1)
            pool.memset(fold[:, :], 0.0).then_inc(consts_made, 1)
            pool.memset(eps[:, :], EPS).then_inc(consts_made, 1)
            pool.wait_ge(consts_made, 5)
            for m in (ident, ident_bf):
                pool.affine_select(out=m[:, :], in_=m[:, :], compare_op=ALU.not_equal, fill=1.0, base=0,
                                   pattern=[[-1, P]], channel_multiplier=1).then_inc(consts_made, 1)
            pool.affine_select(out=causal_bf[:, :], in_=causal_bf[:, :], compare_op=ALU.is_ge, fill=-1e30,
                               base=0, pattern=[[-1, P]], channel_multiplier=1).then_inc(consts_made, 1)
            for half in range(2):
                pool.wait_ge(consts_made, 8 + half)
                pool.affine_select(out=fold[:, :], in_=fold[:, :], compare_op=ALU.not_equal, fill=1.0,
                                   base=-HEAD_DIM * half, pattern=[[-1, HEAD_DIM]],
                                   channel_multiplier=1).then_inc(consts_made, 1)

            def split(u, s, raw_turn):
                raw, parts = w_raw[:, s % RAW_SLOTS, :], w_split[s % WEIGHT_SLOTS]
                pool.wait_ge(raw_in[s % RAW_SLOTS], raw_turn)
                pool.sem_inc(pool_passed, 1)
                pool.tensor_scalar(parts[:, 0, :], raw, 1.0, 1.0, ALU.mult, ALU.mult).then_inc(high_made, 1)
                pool.wait_ge(high_made, u + 1)
                pool.tensor_tensor(parts[:, 1, :], raw, parts[:, 0, :].bitcast(fp32),
                                   ALU.subtract).then_inc(w_ready, 1)

            for s in range(WEIGHT_SLOTS):
                split(s, s, 16 * (s // RAW_SLOTS + 1))
                if s == 1:
                    pool.wait_ge(ws_in, 16)
                    pool.affine_select(out=ws_raw[:, :, :], in_=ws_raw[:, :, :], compare_op=ALU.is_ge,
                                       fill=0.0, base=0, pattern=[[0, GROUPS], [1, CHUNK]],
                                       channel_multiplier=-1).then_inc(ws_masked, 1)
                    pool.wait_ge(ws_masked, 1)
                    pool.tensor_scalar(ws_split[:, 0, :, :], ws_raw[:, :, :], 1.0, 1.0, ALU.mult,
                                       ALU.mult).then_inc(ws_high, 1)
                    pool.wait_ge(ws_high, 1)
                    pool.tensor_tensor(ws_split[:, 1, :, :], ws_raw[:, :, :],
                                       ws_split[:, 0, :, :].bitcast(fp32), ALU.subtract).then_inc(ws_ready, 1)
            with pool.Fori(1, UNITS // WEIGHT_SLOTS) as i:
                for s in range(WEIGHT_SLOTS):
                    pool.wait_ge(w_used, WEIGHT_SLOTS * i + (s + 1 - WEIGHT_SLOTS))
                    split(WEIGHT_SLOTS * i + s, s, 32 * i + 16 * (s // RAW_SLOTS + 1))

        @block.tensor
        def _(pe):
            def products(bank, pairs, first=True, last=True):
                n = len(pairs)
                for j, (a_high, a_low, b_high, b_low) in enumerate(pairs):
                    nc.tensor.matmul(bank, a_high, b_high, start=first and j == 0, stop=False)
                    nc.tensor.matmul(bank, a_low, b_high, start=False, stop=False)
                    mm = nc.tensor.matmul(bank, a_high, b_low, start=False, stop=last and j == n - 1)
                return mm

            def turn(name, rows, after):
                sems = norms[name]
                for t in range(TT):
                    pe.wait_ge(sems["scaled"], t + 1)
                    if t >= 4:
                        pe.wait_ge(sems["split"], t - 3)
                    elif after:
                        after(t)
                    for k in range(KT):
                        mm = nc.tensor.transpose(ps[:, 2 * (t % 4) + k // 4, k % 4 * P:(k % 4 + 1) * P],
                                                 rows[:, t % 4, k * P:(k + 1) * P], ident[:, :])
                    mm.then_inc(sems["turned"], 1)

            def natural(units, first_unit, done, free):
                for u in range(4):
                    slot = w_split[(first_unit + u) % WEIGHT_SLOTS]
                    pe.wait_ge(w_ready, units + u + 1)
                    for kk in range(2):
                        k = 2 * u + kk
                        cols = slice(kk * BANK, (kk + 1) * BANK)
                        for t in range(TT):
                            if k == 0:
                                free(t)
                            tok = slice(t * P, (t + 1) * P)
                            mm = products(ps[:, t, :], [(hn[:, 0, k, tok], hn[:, 1, k, tok],
                                                         slot[:, 0, cols], slot[:, 1, cols])],
                                          first=k == 0, last=k == KT - 1)
                            if k == KT - 1 and t < TT - 1:
                                mm.then_inc(done, 1)
                    mm.then_inc(w_used, 1)

            pe.wait_ge(consts_made, 10)
            turn("pre", xn_first, None)

            pe.wait_ge(norms["pre"]["split"], TT)
            natural(U_GATING, U_GATING, chunk_done, lambda t: None)
            with pe.Fori(1, 3) as i:
                natural(U_GATING + 4 * i, U_GATING, chunk_done,
                        lambda t: pe.wait_ge(chunk_out, TT * i + (t + 1 - TT)))

            pe.wait_ge(ws_ready, 1)
            pe.wait_ge(vn_ready, TT)
            for g in range(GROUPS):
                pe.wait_ge(chunk_out, 2 * TT + g + 1)
                ch = slice(g * GROUP_DIM, (g + 1) * GROUP_DIM)
                products(ps[:, g, :], [(ws_split[:, 0, g, :], ws_split[:, 1, g, :],
                                        vn[:, 0, :, ch], vn[:, 1, :, ch])]).then_inc(spatial_done, 1)

            def column_tile(slot, bank, done, free):
                for half in range(2):
                    free(half)
                    tok = slice(half * BANK, (half + 1) * BANK)
                    mm = products(ps[:, bank + half, :],
                                  [(slot[:, 0, k * P:(k + 1) * P], slot[:, 1, k * P:(k + 1) * P],
                                    hn[:, 0, k, tok], hn[:, 1, k, tok]) for k in range(KT)])
                    mm.then_inc(done if half == 0 else w_used, 1)

            for j in range(4):
                pe.wait_ge(w_ready, U_QK + j + 1)
                column_tile(w_split[j], 2 * j, qk_done, lambda half: pe.wait_ge(spatial_out, 2 * j + half + 1))
            for j in range(4):
                pe.wait_ge(w_ready, U_QK + 4 + j + 1)
                column_tile(w_split[j], 2 * j, qk_done, lambda half: pe.wait_ge(qk_out, 2 * j + half + 1))

            pe.wait_ge(qk_out, 10)
            pe.wait_ge(wf_ready, 1)
            for half in range(2):
                tok = slice(half * BANK, (half + 1) * BANK)
                mm = products(ps[0:HEADS, half, :],
                              [(wf_split[:, 0, k, :], wf_split[:, 1, k, :],
                                hn[:, 0, k, tok], hn[:, 1, k, tok]) for k in range(KT)])
            mm.then_inc(f_done, 1)
            pe.wait_ge(qk_out, 16)
            pe.wait_ge(f_logit, 1)

            def scores(turn_, j):
                a, q = TILES[j]
                if j >= 2:
                    pe.wait_ge(scored, 16 * turn_ + j - 1)
                for c in range(q // 4 + 1):
                    keys = slice(c * BANK, min((q + 1) * P, (c + 1) * BANK))
                    n = keys.stop - keys.start
                    bank = ps[:, 2 * (j % 2) + c, 0:n]
                    own = c == q // 4
                    nc.tensor.matmul(bank, q2[a][:, q * P:(q + 1) * P], k2[a][:, 0, keys], start=True, stop=False)
                    if own:
                        nc.tensor.matmul(ps[:, 2 * (j % 2) + c, n - P:n], ident_bf[:, :], causal_bf[:, :],
                                         start=False, stop=False)
                    mm = nc.tensor.matmul(bank, q2[a][:, q * P:(q + 1) * P], k2[a][:, 1, keys],
                                          start=False, stop=True)
                mm.then_inc(scores_done, 1)

            def move_probs(turn_, j):
                a, q = TILES[j]
                pe.wait_ge(exped, 16 * turn_ + j + 1)
                for part in range(PARTS[j]):
                    n = PART_AT[j] + part
                    if n >= 2:
                        pe.wait_ge(p_split, PART_AT[16] * turn_ + n - 1)
                    for kt in range(4 * part, min(q + 1, 4 * part + 4)):
                        mm = nc.tensor.transpose(ps[:, 4 + n % 2, kt % 4 * P:(kt % 4 + 1) * P],
                                                 probs[:, j % 4, kt * P:(kt + 1) * P], ident[:, :])
                    mm.then_inc(p_moved, 1)

            def values(turn_, m):
                a, blk = divmod(m, TT // 2)
                pe.wait_ge(p_split, PART_AT[16] * turn_ + PART_AT[2 * m + 2])
                if m >= 1:
                    pe.wait_ge(out_t_made, BLOCKS * turn_ + m)
                last = 2 * blk + 1
                part = p_turned[m % 2]

                def high(kt, q0):
                    return nc.tensor.matmul(ps[:, 6, q0:256], v2[:, kt, a, :, :], part[:, 0, kt, q0:256],
                                            start=kt == last, stop=kt == 0, skip_group_check=True)

                def low(kt, q0):
                    nc.tensor.matmul(ps[0:HEAD_DIM, 6, q0:256], v2[:, kt, a, 0, :], part[:, 1, kt, q0:256],
                                     start=False, stop=False, skip_group_check=True)

                high(last, P)
                low(last, P)
                for kt in reversed(range(last)):
                    low(kt, 0)
                    mm = high(kt, 0)
                mm.then_inc(pv_done, 1)

            def fold_out(turn_, m):
                pe.wait_ge(out_t_made, BLOCKS * turn_ + m + 1)
                if m >= 1:
                    pe.wait_ge(attended, BLOCKS * turn_ + m)
                for n in range(2):
                    mm = nc.tensor.matmul(ps[:, 7, n * HEAD_DIM:(n + 1) * HEAD_DIM],
                                          out_t[:, n * P:(n + 1) * P], fold[:, :], start=True, stop=True)
                mm.then_inc(folded, 1)

            with pe.Fori(0, PAIRS) as i:
                pe.wait_ge(heads_ready, i + 1)
                for j in range(len(TILES) + DEPTH):
                    if j < len(TILES):
                        scores(i, j)
                    if 0 <= j - 2 < len(TILES):
                        move_probs(i, j - 2)
                    if j >= 4 and j % 2 == 0 and (j - 4) // 2 < BLOCKS:
                        values(i, (j - 4) // 2)
                    if j >= 5 and j % 2 == 1 and (j - 5) // 2 < BLOCKS:
                        fold_out(i, (j - 5) // 2)
                pe.wait_ge(attended, BLOCKS * i + BLOCKS)

            turn("mix", xn_mix, None)
            pe.wait_ge(norms["mix"]["split"], TT)
            natural(U_MIX, U_MIX, mix_done, lambda t: None)
            natural(U_MIX + 4, U_MIX, mix_done, lambda t: pe.wait_ge(mix_out, t + 1))

            turn("ffn", xn_late, lambda t: pe.wait_ge(mix_out, TT + 2 * t + 2))
            pe.wait_ge(mix_out, 2 * TT)
            pe.wait_ge(norms["ffn"]["split"], TT)

            def inner(unit, slot, done, free):
                pe.wait_ge(w_ready, unit + 1)
                column_tile(w_split[slot % WEIGHT_SLOTS], 0 if done is a_done else 2, done, free)

            def outer(unit, slot, tiles, hid_wait, out_count):
                for o in range(len(tiles)):
                    pe.wait_ge(w_ready, unit + o + 1)
                pe.wait_ge(hid_ready, hid_wait)
                n = 0
                for t in range(TT):
                    tok = slice(t * P, (t + 1) * P)
                    for c in range(2):
                        if out_count is not None or n >= 4:
                            pe.wait_ge(out_added, (0 if out_count is None else out_count) + n - 3)
                        cols = slice(c * BANK, (c + 1) * BANK)
                        mm = products(ps[:, 4 + n % 4, :],
                                      [(hid[s][:, 0, tok], hid[s][:, 1, tok],
                                        w_split[(slot + o) % WEIGHT_SLOTS][:, 0, cols],
                                        w_split[(slot + o) % WEIGHT_SLOTS][:, 1, cols])
                                       for o, s in enumerate(tiles)])
                        n += 1
                        if n < 2 * TT:
                            mm.then_inc(out_done, 1)
                mm.then_inc(w_used, len(tiles))

            def free_a(count):
                return lambda half: pe.wait_ge(a_out, count + half - 1)

            def free_b(count):
                return lambda half: pe.wait_ge(hid_made, count + half - 1)

            inner(U_FFN, 0, a_done, lambda half: None)
            inner(U_FFN + 1, 1, b_done, lambda half: None)
            inner(U_FFN + 2, 2, a_done, free_a(2))
            outer(U_FFN + 3, 3, [0], 2, None)
            inner(U_FFN + 4, 4, b_done, free_b(2))
            with pe.Fori(0, (FT // 2 - 1) // 2) as i:
                for g in range(2):
                    unit, slot = U_FFN + 5 + 12 * i + 6 * g, 5 + 6 * g
                    hidden = 8 * i + 4 * g
                    inner(unit, slot, a_done, free_a(hidden + 4))
                    inner(unit + 1, slot + 1, b_done, free_b(hidden + 4))
                    inner(unit + 2, slot + 2, a_done, free_a(hidden + 6))
                    outer(unit + 3, slot + 3, [1, 0], hidden + 6, 32 * i + 16 * g + 16)
                    inner(unit + 5, slot + 5, b_done, free_b(hidden + 6))
            outer(U_FFN + 3 * FT - 1, 3 * FT - 1, [1], 2 * FT, 16 * (FT // 2))

            turn("gate", xn_late, None)
            pe.wait_ge(norms["gate"]["split"], TT)
            natural(U_GATE, U_GATE, gate_done, lambda t: None)
            natural(U_GATE + 4, U_GATE, gate_done, lambda t: pe.wait_ge(gate_out, t + 1))
            pe.wait_ge(w_ready, U_PLE + 2)
            pe.wait_ge(pt_ready, 1)
            for t in range(TT):
                tok = slice(t * P, (t + 1) * P)
                pe.wait_ge(gate_out, TT + min(2 * (t % 4) + 2, TT))
                if t >= 4:
                    pe.wait_ge(e_scaled, t - 3)
                for c in range(2):
                    mm = products(ps[:, 2 * (t % 4) + c, :],
                                  [(pt_split[:, 0, k, tok], pt_split[:, 1, k, tok],
                                    w_split[(U_PLE + k) % WEIGHT_SLOTS][:, 0, c * BANK:(c + 1) * BANK],
                                    w_split[(U_PLE + k) % WEIGHT_SLOTS][:, 1, c * BANK:(c + 1) * BANK])
                                   for k in range(2)])
                mm.then_inc(ple_done, 1)

        @block.scalar
        def _(act):
            step = Steps(act, act_step)
            act.dma_start(x_tiles[:, 0, :], x[0:P, :]).then_inc(x_in[0], 16)
            act.dma_start(gain[:, 0, :], gains[G_PRE:G_PRE + 1, :].partition_broadcast(P)).then_inc(gain_in, 16)
            for t in range(1, TT):
                act.dma_start(x_tiles[:, t, :], x[t * P:(t + 1) * P, :]).then_inc(x_in[t], 16)
            act.dma_start(ws_raw[:, :, :], ws_t).then_inc(ws_in, 16)
            act.dma_start(gain[:, 1, 0:D_GM], gm_gain.partition_broadcast(P)).then_inc(const_in, 16)
            act.dma_start(bs_col[:, :], b_s).then_inc(const_in, 16)
            act.dma_start(bf_col[0:HEADS, :], b_forget).then_inc(const_in, 16)

            def square(name, norm, t, half, src, junk, scale):
                act.activation(junk, src, ACT.Square, accum_out=stat[:, norm, 0, half, t:t + 1]
                               ).then_inc(norms[name]["squared"], 1)

            def evacuate(name, t):
                act.wait_ge(norms[name]["turned"], t + 1)
                for b in range(2):
                    act.activation(hn[:, 0, 4 * b:4 * b + 4, t * P:(t + 1) * P],
                                   ps[:, 2 * (t % 4) + b, :].rearrange("p (k c) -> p k c", k=4),
                                   ACT.Copy).then_inc(norms[name]["high"], 1)

            act.wait_ge(consts_made, 10)
            for t in range(TT + 2):
                if t < TT:
                    act.wait_ge(x_in[t], 16)
                    if t >= 4:
                        act.wait_ge(norms["pre"]["turned"], t - 3)
                    square("pre", 0, t, 0, x_tiles[:, t, :], xn_first[:, t % 4, :], None)
                    act.wait_ge(norms["pre"]["squared"], t + 1)
                    act.activation(stat[:, 0, 1, 0, t:t + 1], stat[:, 0, 0, 0, t:t + 1], ACT.Sqrt,
                                   bias=eps[:, 0:1], scale=SQRT_ALL).then_inc(norms["pre"]["rooted"], 1)
                if t >= 2:
                    evacuate("pre", t - 2)

            act.wait_ge(norms["pre"]["scaled"], TT)
            for n, dst in enumerate((gv, gu, v_raw)):
                for t in range(TT):
                    chunk_full(act, chunk_done, n, U_GATING, t)
                    act.activation(dst[:, t, :], ps[:, t, :], ACT.Gelu_apprx_tanh if n < 2 else ACT.Copy
                                   ).then_inc(chunk_out, 1)
                if n == 1:
                    act.wait_ge(var_ready, 1)
                    act.activation(g_var[:, :], g_var[:, :], ACT.Sqrt, bias=eps[:, 0:1],
                                   scale=1.0 / GROUP_DIM).then_inc(var_rooted, 1)
                    for t in range(TT):
                        act.wait_ge(vn_scaled, t + 1)
                        act.activation(vn[:, 0, t, :], gv[:, t, :], ACT.Copy).then_inc(vn_high, 1)

            act.wait_ge(ws_ready, 1)
            act.dma_start(wf_raw[:, :, :], w_forget).then_inc(wf_in, 16)

            act.wait_ge(spatial_done, GROUPS)
            with act.Fori(0, 2) as i:
                for j in range(8):
                    pair, which, half = j // 4, j // 2 % 2, j % 2
                    tile_full(act, qk_done, 4 * i + j // 2, U_QK + 4 * i + j // 2, half)
                    act.activation(qk_raw[:, bass.ds(2 * i + pair, 1), which, half * BANK:(half + 1) * BANK]
                                   .rearrange("p a n -> p (a n)"),
                                   ps[:, j, :], ACT.Copy).then_inc(qk_out, 1)

            act.wait_ge(f_logit, 1)
            z, e = forget[0:HEADS, 0, :], forget[0:HEADS, 1, :]
            step(act.activation(e, z, ACT.Abs))
            step(act.activation(e, e, ACT.Exp, scale=-1.0))
            act.activation(e, e, ACT.Ln, bias=1.0).then_inc(f_ln, 1)
            act.wait_ge(c_ready, 1)
            act.dma_start(c_scratch, forget[0:HEADS, 2, :]).then_inc(c_out, 16)
            act.wait_ge(c_out, 16)

            def exps(turn_, j):
                a, q = TILES[j]
                n = (q + 1) * P
                act.wait_ge(scored, 16 * turn_ + j + 1)
                act.activation(probs[:, j % 4, 0:n], probs[:, j % 4, 0:n], ACT.Exp, scale=-1.0,
                               bias=neg_max[:, j:j + 1], accum_out=row_sum[:, j:j + 1]).then_inc(exped, 1)

            def probs_high(turn_, j):
                a, q = TILES[j]
                m = j // 2
                if j % 2 == 0 and m >= 2:
                    act.wait_ge(pv_done, BLOCKS * turn_ + m - 1)
                for part in range(PARTS[j]):
                    n = PART_AT[j] + part
                    act.wait_ge(p_moved, PART_AT[16] * turn_ + n + 1)
                    k0, k1 = 4 * part, min(q + 1, 4 * part + 4)
                    act.activation(p_turned[m % 2][:, 0, k0:k1, q % 2 * P:(q % 2 + 1) * P],
                                   ps[:, 4 + n % 2, 0:(k1 - k0) * P].rearrange("p (k c) -> p k c", c=P),
                                   ACT.Copy).then_inc(p_high, 1)

            def out_t_copy(turn_, m):
                act.wait_ge(pv_done, BLOCKS * turn_ + m + 1)
                if m >= 1:
                    act.wait_ge(folded, BLOCKS * turn_ + m)
                act.activation(out_t[:, :], ps[:, 6, 0:256], ACT.Copy).then_inc(out_t_made, 1)

            with act.Fori(0, PAIRS) as i:
                for a in range(2):
                    act.dma_start(forget_bias[:, a, :],
                                  c_scratch[bass.ds(2 * i + a, 1), :].partition_broadcast(P)
                                  ).then_inc(bias_in, 16)
                pair = bass.ds(i, 1)

                def raw(which, a):
                    return qk_raw[a * HEAD_DIM:(a + 1) * HEAD_DIM, pair, which, :].rearrange("p a n -> p (a n)")

                for a in range(2):
                    own = slice(a * HEAD_DIM, (a + 1) * HEAD_DIM)
                    other = slice((1 - a) * HEAD_DIM, (2 - a) * HEAD_DIM)
                    act.activation(q2[a][own, :], raw(0, a), ACT.Copy).then_inc(heads_high, 1)
                    act.activation(k2[a][own, 0, :], raw(1, a), ACT.Copy).then_inc(heads_high, 1)
                    act.activation(k2[a][other, 0, :], raw(1, a), ACT.Copy).then_inc(heads_high, 1)
                act.activation(v2[:, :, :, 0, :],
                               v_raw[:, :, bass.ds(i * P, P)].rearrange("p t (a c) -> p t a c", a=2),
                               ACT.Copy).then_inc(heads_high, 1)
                for j in range(len(TILES) + DEPTH):
                    if 0 <= j - 2 < len(TILES):
                        probs_high(i, j - 2)
                    if j < len(TILES):
                        exps(i, j)
                    if j >= 4 and j % 2 == 0 and (j - 4) // 2 < BLOCKS:
                        out_t_copy(i, (j - 4) // 2)
                act.wait_ge(attended, BLOCKS * i + BLOCKS)

            act.dma_start(gain[:, 0, :], gains[G_MIX:G_MIX + 1, :].partition_broadcast(P)).then_inc(gain_in, 16)
            act.dma_start(gain[:, 1, :], gains[G_POST:G_POST + 1, :].partition_broadcast(P)).then_inc(gain_in, 16)
            for t in range(TT + 2):
                if t < TT:
                    if t >= 4:
                        act.wait_ge(norms["mix"]["turned"], t - 3)
                    tok = slice(t * P, (t + 1) * P)
                    square("mix", 1, t, 0, qk_raw[:, :, 0, tok],
                           xn_mix[:, t % 4, 0:D_ATT].rearrange("p (a c) -> p a c", a=PAIRS), None)
                    square("mix", 1, t, 1, gu[:, t, :], xn_mix[:, t % 4, D_ATT:], None)
                    act.wait_ge(norms["mix"]["squared"], 2 * t + 2)
                    act.activation(stat[:, 1, 1, :, t:t + 1], stat[:, 1, 0, :, t:t + 1], ACT.Sqrt,
                                   bias=eps[:, 0:1], scale=SQRT_HALF).then_inc(norms["mix"]["rooted"], 1)
                if t >= 2:
                    evacuate("mix", t - 2)
            act.wait_ge(norms["mix"]["scaled"], TT)
            for t in range(TT):
                act.dma_start(h[:, t, :], x[t * P:(t + 1) * P, :]).then_inc(h_in[t], 16)

            act.wait_ge(norms["mix"]["turned"], TT)
            for c in range(2):
                for t in range(TT):
                    chunk_full(act, mix_done, c, U_MIX, t)
                    act.activation(y[:, t, c * BANK:(c + 1) * BANK], ps[:, t, :], ACT.Copy).then_inc(mix_out, 1)

            def post_stats(norm, t, squared, rooted, src, junk):
                act.activation(junk, src, ACT.Square, accum_out=stat[:, norm, 0, 0, t:t + 1]).then_inc(squared, 1)
                act.wait_ge(squared, t + 1)
                act.activation(stat[:, norm, 1, 0, t:t + 1], stat[:, norm, 0, 0, t:t + 1], ACT.Sqrt,
                               bias=eps[:, 0:1], scale=SQRT_ALL).then_inc(rooted, 1)

            def norm_stats(name, norm, t, ready):
                act.wait_ge(ready, t + 1)
                if t >= 4:
                    act.wait_ge(norms[name]["turned"], t - 3)
                square(name, norm, t, 0, h[:, t, :], xn_late[:, t % 4, :], None)
                act.wait_ge(norms[name]["squared"], t + 1)
                act.activation(stat[:, norm, 1, 0, t:t + 1], stat[:, norm, 0, 0, t:t + 1], ACT.Sqrt,
                               bias=eps[:, 0:1], scale=SQRT_ALL).then_inc(norms[name]["rooted"], 1)

            def post_and_norm(name, norm, squared, rooted, ready):
                for t in range(TT + 3):
                    if t < TT:
                        if t >= 4:
                            act.wait_ge(norms[name]["turned"], t - 3)
                        post_stats(norm, t, squared, rooted, y[:, t, :], xn_late[:, t % 4, :])
                    if 1 <= t <= TT:
                        norm_stats(name, norm + 1, t - 1, ready)
                    if t >= 3:
                        evacuate(name, t - 3)

            act.dma_start(gain[:, 0, :], gains[G_FFN:G_FFN + 1, :].partition_broadcast(P)).then_inc(gain_in, 16)
            act.wait_ge(mix_out, 2 * TT)
            post_and_norm("ffn", 2, post_squared, post_rooted, h_ready)
            act.dma_start(gain[:, 1, :], gains[G_FFN_POST:G_FFN_POST + 1, :].partition_broadcast(P)
                          ).then_inc(gain_in, 16)
            act.dma_start(gain[:, 0, :], gains[G_PLE:G_PLE + 1, :].partition_broadcast(P)).then_inc(gain_in, 16)

            def hidden(tile, unit, first=False):
                for half in range(2):
                    tile_full(act, a_done, tile, unit, half)
                    if not first:
                        act.wait_ge(hid_made, 2 * tile + half - 1)
                    act.activation(silu_a[:, half, :], ps[:, half, :], ACT.Silu).then_inc(a_out, 1)

            def hidden_high(slot, tile, outs):
                if outs is not None:
                    act.wait_ge(w_used, outs)
                for half in range(2):
                    act.wait_ge(hid_made, 2 * tile + half + 1)
                    act.activation(hid[slot][:, 0, half * BANK:(half + 1) * BANK], hid_raw[:, half, :],
                                   ACT.Copy).then_inc(hid_high, 1)

            act.wait_ge(norms["ffn"]["turned"], TT)
            hidden(0, U_FFN, True)
            hidden_high(0, 0, None)
            hidden(1, U_FFN + 2)
            hidden_high(1, 1, None)
            with act.Fori(0, (FT // 2 - 1) // 2) as i:
                for g in range(2):
                    tile, unit = 4 * i + 2 * g + 2, U_FFN + 5 + 12 * i + 6 * g
                    hidden(tile, unit)
                    hidden_high(0, tile, unit - 1)
                    hidden(tile + 1, unit + 2)
                    hidden_high(1, tile + 1, unit + 5)

            act.wait_ge(out_added, 16 * (FT // 2 + 1))
            act.dma_start(pt_raw[:, :, :], p_t).then_inc(pt_in, 16)
            post_and_norm("gate", 4, ffn_squared, ffn_rooted, h2_ready)

            act.wait_ge(pt_in, 16)
            act.activation(pt_split[:, 0, :, :], pt_raw[:, :, :], ACT.Copy).then_inc(pt_high, 1)
            for c in range(2):
                for t in range(TT):
                    chunk_full(act, gate_done, c, U_GATE, t)
                    act.activation(y[:, t, c * BANK:(c + 1) * BANK], ps[:, t, :], ACT.Sigmoid).then_inc(gate_out, 1)
            for t in range(TT):
                act.wait_ge(ple_done, t + 1)
                if t >= 2:
                    act.wait_ge(row_ready, t - 1)
                else:
                    act.wait_ge(pt_ready, 1)
                pair_of_banks = ps[:, 2 * (t % 4):2 * (t % 4) + 2, :]
                e_t = e_tile[:, t % 2, :]
                act.activation(e_t.rearrange("p (b c) -> p b c", b=2), pair_of_banks, ACT.Square,
                               accum_out=stat[:, 6, 0, 0, t:t + 1]).then_inc(e_squared, 1)
                act.wait_ge(e_squared, t + 1)
                act.activation(stat[:, 6, 1, 0, t:t + 1], stat[:, 6, 0, 0, t:t + 1], ACT.Sqrt,
                               bias=eps[:, 0:1], scale=SQRT_ALL).then_inc(e_rooted, 1)

        @block.vector
        def _(dve):
            step = Steps(dve, dve_step)

            def low_parts(name, t):
                for b in range(2):
                    dve.wait_ge(norms[name]["high"], 2 * t + b + 1)
                    hi = hn[:, 0, 4 * b:4 * b + 4, t * P:(t + 1) * P].bitcast(fp32)
                    ins = dve.tensor_tensor(hn[:, 1, 4 * b:4 * b + 4, t * P:(t + 1) * P],
                                            ps[:, 2 * (t % 4) + b, :].rearrange("p (k c) -> p k c", k=4),
                                            hi, ALU.subtract)
                ins.then_inc(norms[name]["split"], 1)

            def inverse(norm, t, halves=1):
                step(dve.reciprocal(stat[:, norm, 2, 0:halves, t:t + 1], stat[:, norm, 1, 0:halves, t:t + 1]))

            dve.wait_ge(gain_in, 16)
            dve.wait_ge(const_in, 16 * 3)
            for t in range(TT + 2):
                if t < TT:
                    dve.wait_ge(norms["pre"]["rooted"], t + 1)
                    inverse(0, t)
                    dve.scalar_tensor_tensor(out=xn_first[:, t % 4, :], in0=x_tiles[:, t, :],
                                             scalar=stat[:, 0, 2, 0, t:t + 1], in1=gain[:, 0, :],
                                             op0=ALU.mult, op1=ALU.mult).then_inc(norms["pre"]["scaled"], 1)
                if t >= 2:
                    low_parts("pre", t - 2)

            for t in range(TT):
                dve.wait_ge(chunk_out, t + 1)
                groups = gv[:, t, :].rearrange("p (g c) -> p g c", g=GROUPS)
                gs = slice(t * GROUPS, (t + 1) * GROUPS)
                step(dve.tensor_reduce(g_sum[:, gs], groups, AX.X, ALU.add))
                step(dve.tensor_scalar(g_sum[:, gs], g_sum[:, gs], -1.0 / GROUP_DIM, None, ALU.mult))
                step(dve.tensor_tensor(groups, groups, g_sum[:, gs].unsqueeze(2).broadcast_to([P, GROUPS, GROUP_DIM]),
                                       ALU.add))
                sq = squares[:, t % 2, :]
                step(dve.tensor_tensor(sq, gv[:, t, :], gv[:, t, :], ALU.mult))
                ins = dve.tensor_reduce(g_var[:, gs], sq.rearrange("p (g c) -> p g c", g=GROUPS), AX.X, ALU.add)
                if t < TT - 1:
                    step(ins)
            ins.then_inc(var_ready, 1)
            dve.wait_ge(var_rooted, 1)
            step(dve.reciprocal(g_inv[:, :], g_var[:, :]))
            for t in range(TT + 1):
                if t < TT:
                    groups = gv[:, t, :].rearrange("p (g c) -> p g c", g=GROUPS)
                    gs = slice(t * GROUPS, (t + 1) * GROUPS)
                    step(dve.tensor_tensor(groups, groups,
                                           g_inv[:, gs].unsqueeze(2).broadcast_to([P, GROUPS, GROUP_DIM]),
                                           ALU.mult))
                    dve.tensor_tensor(gv[:, t, :], gv[:, t, :], gain[:, 1, 0:D_GM], ALU.mult).then_inc(vn_scaled, 1)
                if t >= 1:
                    dve.wait_ge(vn_high, t)
                    dve.tensor_tensor(vn[:, 1, t - 1, :], gv[:, t - 1, :], vn[:, 0, t - 1, :].bitcast(fp32),
                                      ALU.subtract).then_inc(vn_ready, 1)

            dve.wait_ge(wf_in, 16)
            step(dve.tensor_copy(wf_split[:, 0, :, :], wf_raw[:, :, :]))
            dve.tensor_tensor(wf_split[:, 1, :, :], wf_raw[:, :, :], wf_split[:, 0, :, :].bitcast(fp32),
                              ALU.subtract).then_inc(wf_ready, 1)

            for g in range(GROUPS):
                dve.wait_ge(spatial_done, g + 1)
                ch = slice(g * GROUP_DIM, (g + 1) * GROUP_DIM)
                dve.scalar_tensor_tensor(out=gu[:, :, ch], in0=ps[:, g, :].rearrange("p (n c) -> p n c", n=TT),
                                         scalar=bs_col[:, g:g + 1], in1=gu[:, :, ch],
                                         op0=ALU.add, op1=ALU.mult).then_inc(spatial_out, 1)

            z, ln1p, c_row = forget[0:HEADS, 0, :], forget[0:HEADS, 1, :], forget[0:HEADS, 2, :]
            dve.wait_ge(f_done, 1)
            dve.wait_ge(vn_high, TT)
            dve.wait_ge(vn_ready, TT)
            dve.tensor_scalar(z.rearrange("p (b c) -> p b c", b=2), ps[0:HEADS, 0:2, :], bf_col[0:HEADS, 0:1], None,
                              ALU.add).then_inc(f_logit, 1)
            dve.wait_ge(f_logit, 1)
            dve.wait_ge(f_ln, 1)
            step(dve.scalar_tensor_tensor(out=ln1p, in0=z, scalar=0.0, in1=ln1p, op0=ALU.min, op1=ALU.subtract))
            step(dve.memset(z, 0.0))
            step(dve.tensor_tensor_scan(c_row, ln1p, z, 0.0, ALU.add, ALU.add))
            dve.tensor_scalar(c_row, c_row, -float(HEAD_DIM) ** 0.5, None, ALU.mult).then_inc(c_ready, 1)

            def score(turn_, j):
                a, q = TILES[j]
                n = (q + 1) * P
                dve.wait_ge(scores_done, 16 * turn_ + j + 1)
                if j >= 4:
                    dve.wait_ge(p_moved, PART_AT[16] * turn_ + PART_AT[j - 3])
                dve.sem_inc(dve_passed, 1)
                src = ps[:, 2 * (j % 2):2 * (j % 2) + 2, :].rearrange("p b c -> p (b c)")[:, 0:n]
                dve.tensor_tensor_reduce(probs[:, j % 4, 0:n], src, forget_bias[:, a, 0:n],
                                         -float(HEAD_DIM) ** -0.5, 3e38, ALU.add, ALU.min,
                                         neg_max[:, j:j + 1]).then_inc(scored, 1)

            def probs_low(turn_, j):
                a, q = TILES[j]
                for part in range(PARTS[j]):
                    n = PART_AT[j] + part
                    dve.wait_ge(p_high, PART_AT[16] * turn_ + n + 1)
                    k0, k1 = 4 * part, min(q + 1, 4 * part + 4)
                    cols = slice(q % 2 * P, (q % 2 + 1) * P)
                    both = p_turned[j // 2 % 2]
                    dve.tensor_tensor(both[:, 1, k0:k1, cols],
                                      ps[:, 4 + n % 2, 0:(k1 - k0) * P].rearrange("p (k c) -> p k c", c=P),
                                      both[:, 0, k0:k1, cols].bitcast(fp32), ALU.subtract).then_inc(p_split, 1)

            def attend(turn_, m, pair):
                a, blk = divmod(m, TT // 2)
                dve.wait_ge(exped, 16 * turn_ + 2 * m + 2)
                step(dve.reciprocal(row_inv[:, 2 * m:2 * m + 2], row_sum[:, 2 * m:2 * m + 2]))
                dve.wait_ge(folded, BLOCKS * turn_ + m + 1)
                for n in range(2):
                    t = 2 * blk + n
                    col = t * P + a * HEAD_DIM
                    ins = dve.tensor_scalar(qk_raw[:, pair, 0, col:col + HEAD_DIM].rearrange("p a n -> p (a n)"),
                                            ps[:, 7, n * HEAD_DIM:(n + 1) * HEAD_DIM],
                                            row_inv[:, 2 * m + n:2 * m + n + 1], None, ALU.mult)
                ins.then_inc(attended, 1)

            with dve.Fori(0, PAIRS) as i:
                pair = bass.ds(i, 1)
                step.loop(i, BLOCKS)

                def raw(which, a):
                    return qk_raw[a * HEAD_DIM:(a + 1) * HEAD_DIM, pair, which, :].rearrange("p a n -> p (a n)")

                for a in range(2):
                    own = slice(a * HEAD_DIM, (a + 1) * HEAD_DIM)
                    other = slice((1 - a) * HEAD_DIM, (2 - a) * HEAD_DIM)
                    dve.wait_ge(heads_high, 7 * i + 3 * a + 2)
                    dve.tensor_tensor(q2[a][other, :], raw(0, a), q2[a][own, :].bitcast(fp32), ALU.subtract)
                    dve.tensor_tensor(k2[a][own, 1, :], raw(1, a), k2[a][own, 0, :].bitcast(fp32), ALU.subtract)
                    dve.tensor_tensor(k2[a][other, 1, :], raw(1, a), k2[a][own, 0, :].bitcast(fp32), ALU.subtract)
                dve.wait_ge(heads_high, 7 * i + 7)
                dve.tensor_tensor(v2[:, :, :, 1, :],
                                  v_raw[:, :, bass.ds(i * P, P)].rearrange("p t (a c) -> p t a c", a=2),
                                  v2[:, :, :, 0, :].bitcast(fp32), ALU.subtract).then_inc(heads_ready, 1)
                dve.wait_ge(bias_in, 32 * i + 32)
                dve.wait_ge(heads_ready, i + 1)
                for j in range(len(TILES) + DEPTH):
                    if j < len(TILES):
                        score(i, j)
                    if 0 <= j - 2 < len(TILES):
                        probs_low(i, j - 2)
                    if j >= 5 and j % 2 == 1 and (j - 5) // 2 < BLOCKS:
                        attend(i, (j - 5) // 2, pair)
                dve.wait_ge(attended, BLOCKS * i + BLOCKS)
                step.end_loop(PAIRS)

            dve.wait_ge(gain_in, 48)
            for t in range(TT + 2):
                if t < TT:
                    dve.wait_ge(norms["mix"]["rooted"], t + 1)
                    inverse(1, t, 2)
                    tok = slice(t * P, (t + 1) * P)
                    for half, src in enumerate((qk_raw[:, :, 0, tok], gu[:, t, :])):
                        cols = slice(half * D_ATT, (half + 1) * D_ATT)
                        dst, g = xn_mix[:, t % 4, cols], gain[:, 0, cols]
                        if half == 0:
                            dst = dst.rearrange("p (a c) -> p a c", a=PAIRS)
                            g = g.rearrange("p (a c) -> p a c", a=PAIRS)
                        ins = dve.scalar_tensor_tensor(out=dst, in0=src, scalar=stat[:, 1, 2, half, t:t + 1],
                                                       in1=g, op0=ALU.mult, op1=ALU.mult)
                    ins.then_inc(norms["mix"]["scaled"], 1)
                if t >= 2:
                    low_parts("mix", t - 2)

            def post(norm, t, rooted, ready):
                dve.wait_ge(rooted, t + 1)
                inverse(norm, t)
                step(dve.scalar_tensor_tensor(out=y[:, t, :], in0=y[:, t, :], scalar=stat[:, norm, 2, 0, t:t + 1],
                                              in1=gain[:, 1, :], op0=ALU.mult, op1=ALU.mult))
                dve.tensor_tensor(h[:, t, :], h[:, t, :], y[:, t, :], ALU.add).then_inc(ready, 1)

            def scale_rows(name, norm, t, with_gain, ready):
                dve.wait_ge(norms[name]["rooted"], t + 1)
                inverse(norm, t)
                dst, r = xn_late[:, t % 4, :], stat[:, norm, 2, 0, t:t + 1]
                if with_gain:
                    ins = dve.scalar_tensor_tensor(out=dst, in0=h[:, t, :], scalar=r, in1=gain[:, 0, :],
                                                   op0=ALU.mult, op1=ALU.mult)
                else:
                    ins = dve.tensor_scalar(dst, h[:, t, :], r, None, ALU.mult)
                ins.then_inc(norms[name]["scaled"], 1)

            for t in range(TT + 3):
                if t < TT:
                    dve.wait_ge(h_in[t], 16)
                    post(2, t, post_rooted, h_ready)
                if 1 <= t <= TT:
                    if t == 1:
                        dve.wait_ge(gain_in, 64)
                    scale_rows("ffn", 3, t - 1, True, h_ready)
                if t >= 3:
                    low_parts("ffn", t - 3)

            def hidden(slot, tile, unit):
                for half in range(2):
                    cols = slice(half * BANK, (half + 1) * BANK)
                    tile_full(dve, b_done, tile, unit, half)
                    dve.wait_ge(a_out, 2 * tile + half + 1)
                    dve.tensor_tensor(hid_raw[:, half, :], ps[:, 2 + half, :], silu_a[:, half, :],
                                      ALU.mult).then_inc(hid_made, 1)
                for half in range(2):
                    cols = slice(half * BANK, (half + 1) * BANK)
                    dve.wait_ge(hid_high, 2 * tile + half + 1)
                    dve.tensor_tensor(hid[slot][:, 1, cols], hid_raw[:, half, :],
                                      hid[slot][:, 0, cols].bitcast(fp32), ALU.subtract).then_inc(hid_ready, 1)
                dve.wait_ge(hid_ready, 2 * tile + 2)

            def add_out(turn_, last_unit, copy=False):
                for n in range(2 * TT):
                    t, cols = n // 2, slice(n % 2 * BANK, (n % 2 + 1) * BANK)
                    if n < 2 * TT - 1:
                        dve.wait_ge(out_done, (2 * TT - 1) * turn_ + n + 1)
                    else:
                        dve.wait_ge(w_used, last_unit + 1)
                    if copy:
                        dve.tensor_copy(y[:, t, cols], ps[:, 4 + n % 4, :]).then_inc(out_added, 1)
                    else:
                        dve.tensor_tensor(y[:, t, cols], ps[:, 4 + n % 4, :], y[:, t, cols],
                                          ALU.add).then_inc(out_added, 1)

            dve.wait_ge(h_ready, TT)
            hidden(0, 0, U_FFN + 1)
            add_out(0, U_FFN + 3, copy=True)
            hidden(1, 1, U_FFN + 4)
            with dve.Fori(0, (FT // 2 - 1) // 2) as i:
                for g in range(2):
                    tile, unit = 4 * i + 2 * g + 2, U_FFN + 5 + 12 * i + 6 * g
                    hidden(0, tile, unit + 1)
                    dve.wait_ge(out_added, 32 * i + 16 * g + 16)
                    add_out(2 * i + g + 1, unit + 4)
                    hidden(1, tile + 1, unit + 5)
            dve.wait_ge(out_added, 16 * (FT // 2))
            add_out(FT // 2, U_FFN + 3 * FT - 1)

            dve.wait_ge(gain_in, 96)
            for t in range(TT + 3):
                if t < TT:
                    post(4, t, ffn_rooted, h2_ready)
                if 1 <= t <= TT:
                    scale_rows("gate", 5, t - 1, False, h2_ready)
                if t >= 3:
                    low_parts("gate", t - 3)
            dve.wait_ge(pt_high, 1)
            dve.tensor_tensor(pt_split[:, 1, :, :], pt_raw[:, :, :], pt_split[:, 0, :, :].bitcast(fp32),
                              ALU.subtract).then_inc(pt_ready, 1)

            for t in range(TT):
                dve.wait_ge(e_rooted, t + 1)
                inverse(6, t)
                e_t = e_tile[:, t % 2, :]
                banks = ps[:, 2 * (t % 4):2 * (t % 4) + 2, :].rearrange("p b c -> p (b c)")
                ins = dve.scalar_tensor_tensor(out=e_t, in0=banks, scalar=stat[:, 6, 2, 0, t:t + 1],
                                               in1=gain[:, 0, :], op0=ALU.mult, op1=ALU.mult)
                ins.then_inc(e_scaled, 1)
                dve.wait_ge(e_scaled, t + 1)
                dve.wait_ge(gate_out, 2 * TT)
                step(dve.tensor_tensor(e_t, e_t, y[:, t, :], ALU.mult))
                dve.tensor_tensor(h[:, t, :], h[:, t, :], e_t, ALU.add).then_inc(row_ready, 1)


def kernel(x, p, mix_pre_norm, mix_post_norm, w_in, b_forget, gm_v_norm, gm_w_s, gm_b_s, mix_out_norm,
           w_out, ffn_pre_norm, ffn_post_norm, w_ffn_in, w_ffn_out, w_ple, ple_norm, w_ple_gate):
    import concourse.bacc as bacc
    from concourse.bass_utils import run_bass_kernel_spmd

    f = lambda a: np.asarray(a)
    w_in, w_out, w_ffn_in, w_ffn_out, w_ple, w_gate = (
        f(a)[0] for a in (w_in, w_out, w_ffn_in, w_ffn_out, w_ple, w_ple_gate))

    def chunk(w):
        return w.reshape(-1, 2, P, BANK).transpose(0, 2, 1, 3).reshape(-1, P, UNIT)

    def columns(w):
        return w.reshape(1, KT, P, P).transpose(0, 2, 1, 3).reshape(1, P, UNIT)

    q0, k0, v0 = 0, D_ATT, 2 * D_ATT
    f0 = 3 * D_ATT
    g0 = f0 + HEADS
    units = [chunk(w_in[:, g0 + D_GM:]), chunk(w_in[:, g0:g0 + D_GM]), chunk(w_in[:, v0:v0 + D_ATT])]
    for pair in range(PAIRS):
        units += [columns(w_in[:, c + pair * P:c + (pair + 1) * P]) for c in (q0, k0)]
    units += [chunk(w_out[:, :BANK]), chunk(w_out[:, BANK:])]
    a = [columns(w_ffn_in[:, j * P:(j + 1) * P]) for j in range(FT)]
    b = [columns(w_ffn_in[:, D_FF + j * P:D_FF + (j + 1) * P]) for j in range(FT)]
    o = [w_ffn_out[None, j * P:(j + 1) * P, :] for j in range(FT)]
    for j in range(0, FT, 2):
        units += [a[j], b[j], a[j + 1], *o[max(j - 1, 0):j + 1], b[j + 1]]
    units += [o[FT - 1], chunk(w_gate[:, :BANK]), chunk(w_gate[:, BANK:]), w_ple.reshape(2, P, UNIT)]
    packed = np.concatenate(units, axis=0)
    assert packed.shape[0] == UNITS

    arrays = {
        "x": f(x)[0],
        "weights": packed,
        "w_forget": w_in[:, f0:g0].reshape(KT, P, HEADS).transpose(1, 0, 2),
        "b_forget": f(b_forget)[0][:, None],
        "p_t": f(p)[0, 0].T.reshape(2, P, TOKENS).transpose(1, 0, 2),
        "ws_t": f(gm_w_s)[0].transpose(2, 0, 1),
        "b_s": f(gm_b_s)[0].T,
        "gains": np.stack([f(g)[0] for g in (mix_pre_norm, mix_out_norm, mix_post_norm, ffn_pre_norm,
                                             ffn_post_norm, ple_norm)]),
        "gm_gain": f(gm_v_norm),
    }
    nc = bacc.Bacc("TRN2", target_bir_lowering=False, num_devices=1)
    fp32 = mybir.dt.float32
    aps = {}
    for name, value in arrays.items():
        arrays[name] = value = np.ascontiguousarray(value)
        aps[name] = nc.dram_tensor(name, value.shape, mybir.dt.from_np(value.dtype), kind="ExternalInput").ap()
    c_scratch = nc.dram_tensor("c_scratch", (HEADS, TOKENS), fp32).ap()
    out = nc.dram_tensor("out", (TOKENS, D_MODEL), fp32, kind="ExternalOutput").ap()
    build_trunk(nc, c_scratch=c_scratch, out=out, **aps)
    result = run_bass_kernel_spmd(nc, [arrays], core_ids=[0])
    return result.results[0]["out"].reshape(1, TOKENS, D_MODEL)
```

```python
import concourse.bass as bass
import numpy as np
from concourse import mybir

TOKENS, D_MODEL = 1024, 1024
HEADS, HEAD_DIM = 8, 64
D_ATT = HEADS * HEAD_DIM
GROUPS, GROUP_DIM, CHUNK = 8, 64, 128
D_GM = GROUPS * GROUP_DIM
D_FF = ((8 * D_MODEL // 3 + 255) // 256) * 256
PLE_DIM = 256
EPS = 1e-6

P = 128
TT = TOKENS // P
KT = D_MODEL // P
FT = D_FF // P
PAIRS = HEADS // 2
BANK = 512
UNIT = 1024
NT_COLS = D_MODEL // P

U_GATING, U_QK, U_MIX = 0, 12, 20
U_FFN = U_MIX + 8
U_PLE = U_FFN + 3 * FT
U_GATE = U_PLE + 2
UNITS = U_GATE + 8
RAW_SLOTS, WEIGHT_SLOTS = 2, 4


class Steps:

    def __init__(self, engine, semaphore):
        self.engine, self.semaphore, self.done, self.turn = engine, semaphore, 0, 0

    def __call__(self, instruction):
        instruction.then_inc(self.semaphore, 1)
        self.done += 1
        self.engine.wait_ge(self.semaphore, self.turn + self.done)

    def loop(self, i, per):
        self.start, self.per, self.turn = self.done, per, i * per

    def end_loop(self, turns):
        assert self.done - self.start == self.per
        self.done, self.turn = self.start + turns * self.per, 0


def build_trunk(nc, x, weights, w_forget, b_forget, p_t, ws_t, b_s, gains, gm_gain, c_scratch, out):
    fp32, fp32r, bf16 = mybir.dt.float32, mybir.dt.float32r, mybir.dt.bfloat16
    ALU, ACT, AX = mybir.AluOpType, mybir.ActivationFunctionType, mybir.AxisListType

    KB = 1024
    base = (nc.sbuf_base + 63) // 64 * 64
    at = {"ring": base, "raw": base + 32 * KB, "gain": base + 40 * KB, "hn": base + 48 * KB,
          "f": base + 112 * KB, "small": base + 204 * KB}

    def place(name, shape, dtype, region, kb=0.0):
        return nc.alloc_sbuf_tensor_at(name, [P, *shape], dtype, offset=at[region] + int(kb * KB))

    w_raw = place("w_raw", [RAW_SLOTS, UNIT], fp32, "raw")
    w_split = [place(f"w_split{s}", [2, UNIT], fp32r, "ring", 8 * s) for s in range(WEIGHT_SLOTS)]
    gain = place("gain", [2, D_MODEL], fp32, "gain")
    hn = place("hn", [2, KT, TOKENS], fp32r, "hn")

    x_tiles = place("x_tiles", [TT, D_MODEL], fp32, "f", 0)
    xn_first = place("xn_first", [4, D_MODEL], fp32, "f", 48)
    gv = place("gv", [TT, D_GM], fp32, "f", 0)
    gu = place("gu", [TT, D_GM], fp32, "f", 16)
    v_raw = place("v_raw", [TT, D_ATT], fp32, "f", 32)
    vn = place("vn", [2, TT, D_GM], fp32r, "f", 48)
    qk_raw = place("qk_raw", [PAIRS, 2, TOKENS], fp32, "f", 48)
    junk_first = place("junk_first", [D_MODEL], bf16, "f", 32)
    squares = place("squares", [2, D_GM], fp32, "f", 48)
    ws_split = place("ws_split", [2, GROUPS, CHUNK], fp32r, "f", 80)
    ws_raw = place("ws_raw", [GROUPS, CHUNK], fp32, "f", 88)

    p_turned = [place(f"p_turned{s}", [2, TT, 256], fp32r, "hn", 16 * s) for s in range(2)]
    q2 = [place(f"q2_{a}", [TOKENS], fp32r, "hn", 32 + 4 * a) for a in range(2)]
    k2 = [place(f"k2_{a}", [2, TOKENS], fp32r, "hn", 40 + 8 * a) for a in range(2)]
    v2 = place("v2", [TT, 2, 2, HEAD_DIM], fp32r, "hn", 56)
    probs = place("probs", [4, TOKENS], fp32, "f", 0)
    forget_bias = place("forget_bias", [2, TOKENS], fp32, "f", 80)
    out_t = place("out_t", [256], fp32, "f", 88)
    forget = place("forget", [4, TOKENS], fp32, "f", 0)
    wf_raw = place("wf_raw", [KT, HEADS], fp32, "f", 89)
    wf_split = place("wf_split", [2, KT, HEADS], fp32r, "f", 89.5)

    xn_mix = place("xn_mix", [4, D_MODEL], fp32, "f", 0)
    y = place("y", [TT, D_MODEL], fp32, "f", 0)
    h = place("h", [TT, D_MODEL], fp32, "f", 32)
    xn_ffn = place("xn_ffn", [4, D_MODEL], fp32, "f", 64)
    xn_gate = place("xn_gate", [2, D_MODEL], fp32, "f", 80)
    junk = place("junk", [D_MODEL], bf16, "f", 88)
    hid = [place(f"hid{s}", [2, TOKENS], fp32r, "f", 64 + 8 * s) for s in range(2)]
    silu_a = place("silu_a", [2, BANK], fp32, "f", 80)
    hid_raw = place("hid_raw", [2, BANK], fp32, "f", 84)
    pt_raw = place("pt_raw", [2, TOKENS], fp32, "hn", 0)
    pt_split = [place(f"pt_split{k}", [2, TOKENS], fp32r, "f", 64 + 8 * k) for k in range(2)]
    gates = place("gates", [8, BANK], fp32, "f", 64)

    ident = place("ident", [P], fp32, "small", 0)
    ident_bf = place("ident_bf", [P], bf16, "small", 0.5)
    causal_bf = place("causal_bf", [P], bf16, "small", 0.75)
    fold = place("fold", [HEAD_DIM], fp32, "small", 1)
    bs_col = place("bs_col", [GROUPS], fp32, "small", 1.25)
    bf_col = place("bf_col", [1], fp32, "small", 1.3125)
    row_sum = place("row_sum", [2 * TT], fp32, "small", 1.375)
    row_inv = place("row_inv", [2 * TT], fp32, "small", 1.5)
    neg_max = place("neg_max", [2 * TT], fp32, "small", 1.625)
    g_sum = place("g_sum", [TT * GROUPS], fp32, "small", 1.75)
    g_var = place("g_var", [TT * GROUPS], fp32, "small", 2)
    g_inv = place("g_inv", [TT * GROUPS], fp32, "small", 2.25)
    stat = place("stat", [7, 3, 2, TT], fp32, "small", 2.5)
    eps = place("eps", [1], fp32, "small", 3.8125)
    ps = nc.alloc_psum_tensor("ps", [P, 8, BANK], fp32)

    def sem(name):
        return nc.alloc_semaphore(name)

    raw_in = [sem(f"raw_in{s}") for s in range(RAW_SLOTS)]
    high_made, w_ready, w_used = sem("high_made"), sem("w_ready"), sem("w_used")
    x_in = [sem(f"x_in{t}") for t in range(TT)]
    h_in = [sem(f"h_in{t}") for t in range(TT)]
    const_in, ws_in, pt_in, gain_in = sem("const_in"), sem("ws_in"), sem("pt_in"), sem("gain_in")
    pool_passed, dve_passed = sem("pool_passed"), sem("dve_passed")
    consts_made, wf_in, wf_ready = sem("consts_made"), sem("wf_in"), sem("wf_ready")
    ws_masked, ws_high, ws_ready = sem("ws_masked"), sem("ws_high"), sem("ws_ready")
    dve_step, act_step = sem("dve_step"), sem("act_step")
    norms = {n: {k: sem(f"norm_{n}_{k}") for k in ("squared", "rooted", "scaled", "turned", "high", "split")}
             for n in ("pre", "mix", "ffn", "gate")}
    chunk_done, chunk_out = sem("chunk_done"), sem("chunk_out")
    var_ready, var_rooted, vn_scaled, vn_high, vn_ready = (
        sem("var_ready"), sem("var_rooted"), sem("vn_scaled"), sem("vn_high"), sem("vn_ready"))
    spatial_done, spatial_out = sem("spatial_done"), sem("spatial_out")
    qk_done, qk_out, f_done, f_logit, f_exp, f_ln, c_ready, c_out = (
        sem("qk_done"), sem("qk_out"), sem("f_done"), sem("f_logit"), sem("f_exp"), sem("f_ln"),
        sem("c_ready"), sem("c_out"))
    bias_in = [sem(f"bias_in{a}") for a in range(2)]
    heads_high, heads_ready = sem("heads_high"), sem("heads_ready")
    scores_done, scored, exped, p_moved, p_high, p_split = (
        sem("scores_done"), sem("scored"), sem("exped"), sem("p_moved"), sem("p_high"), sem("p_split"))
    pv_done, out_t_made, folded, attended = sem("pv_done"), sem("out_t_made"), sem("folded"), sem("attended")
    mix_done, mix_out = sem("mix_done"), sem("mix_out")
    post_squared, post_rooted, h_ready = sem("post_squared"), sem("post_rooted"), sem("h_ready")
    a_done, a_out, b_done, hid_made, hid_high, hid_ready, out_done, out_added = (
        sem("a_done"), sem("a_out"), sem("b_done"), sem("hid_made"), sem("hid_high"),
        sem("hid_ready"), sem("out_done"), sem("out_added"))
    ffn_squared, ffn_rooted, h2_ready = sem("ffn_squared"), sem("ffn_rooted"), sem("h2_ready")
    h_posted, h2_posted = sem("h_posted"), sem("h2_posted")
    gate_done, gate_out, pt_high, pt_ready = sem("gate_done"), sem("gate_out"), sem("pt_high"), sem("pt_ready")
    ple_done, e_out, e_squared, e_rooted, e_scaled, row_ready, stored = (
        sem("ple_done"), sem("e_out"), sem("e_squared"), sem("e_rooted"), sem("e_scaled"),
        sem("row_ready"), sem("stored"))

    G_PRE, G_MIX, G_POST, G_FFN, G_FFN_POST, G_PLE = range(6)
    SQRT_ALL, SQRT_HALF = 1.0 / D_MODEL, 1.0 / D_ATT

    TILES = [(a, q) for a in range(2) for q in range(TT)]
    PARTS = [q // 4 + 1 for _, q in TILES]
    PART_AT = [sum(PARTS[:j]) for j in range(len(TILES) + 1)]
    BLOCKS = len(TILES) // 2
    N_TILES, N_PARTS = len(TILES), PART_AT[-1]
    DEPTH = 5
    SPLIT_AT = {0: (1, 0), 1: (1, 1), 2: (1, 2), 4: (1, 3), 8: (0, 0), 9: (0, 1), 10: (0, 2), 11: (0, 3)}
    SPLITS = 4

    def lagged(turn, j, lag):
        if j >= lag:
            return (turn, j - lag) if j - lag < N_TILES else None
        return None if is_first(turn) else (turn - 1, j - lag + N_TILES)

    def is_first(turn):
        return isinstance(turn, int) and turn == 0

    def pairs_of_heads(engine, body):
        body(0, N_TILES)
        with engine.Fori(1, PAIRS - 1) as i:
            body(i, N_TILES)
        body(PAIRS - 1, N_TILES + DEPTH)

    def chunk_full(engine, done, chunk, first_unit, t):
        if t < TT - 1:
            engine.wait_ge(done, (TT - 1) * chunk + t + 1)
        else:
            engine.wait_ge(w_used, first_unit + 4 * chunk + 4)

    def tile_full(engine, done, tiles, unit, half):
        if half == 0:
            engine.wait_ge(done, tiles + 1)
        else:
            engine.wait_ge(w_used, unit + 1)

    block = nc.Block()
    with block:

        @block.sync
        def _(sp):
            for s in range(RAW_SLOTS):
                sp.dma_start(w_raw[:, s, :], weights[s]).then_inc(raw_in[s], 16)
            with sp.Fori(1, UNITS // RAW_SLOTS) as i:
                for s in range(RAW_SLOTS):
                    sp.wait_ge(w_ready, RAW_SLOTS * i + (s + 1 - RAW_SLOTS))
                    sp.dma_start(w_raw[:, s, :], weights[bass.ds(RAW_SLOTS * i + s, 1)][0]
                                 ).then_inc(raw_in[s], 16)
            for n in range(2 * TT):
                t, cols = n % TT, slice(n // TT * BANK, (n // TT + 1) * BANK)
                sp.wait_ge(row_ready, n + 1)
                sp.dma_start(out[t * P:(t + 1) * P, cols], h[:, t, cols]).then_inc(stored, 16)
            sp.wait_ge(stored, 16 * 2 * TT)

        @block.gpsimd
        def _(pool):
            pool.memset(ident[:, :], 0.0).then_inc(consts_made, 1)
            pool.memset(ident_bf[:, :], 0.0).then_inc(consts_made, 1)
            pool.memset(causal_bf[:, :], 0.0).then_inc(consts_made, 1)
            pool.memset(fold[:, :], 0.0).then_inc(consts_made, 1)
            pool.memset(eps[:, :], EPS).then_inc(consts_made, 1)
            pool.wait_ge(consts_made, 5)
            for m in (ident, ident_bf):
                pool.affine_select(out=m[:, :], in_=m[:, :], compare_op=ALU.not_equal, fill=1.0, base=0,
                                   pattern=[[-1, P]], channel_multiplier=1).then_inc(consts_made, 1)
            pool.affine_select(out=causal_bf[:, :], in_=causal_bf[:, :], compare_op=ALU.is_ge, fill=-1e30,
                               base=0, pattern=[[-1, P]], channel_multiplier=1).then_inc(consts_made, 1)
            for half in range(2):
                pool.wait_ge(consts_made, 8 + half)
                pool.affine_select(out=fold[:, :], in_=fold[:, :], compare_op=ALU.not_equal, fill=1.0,
                                   base=-HEAD_DIM * half, pattern=[[-1, HEAD_DIM]],
                                   channel_multiplier=1).then_inc(consts_made, 1)

            def split(u, s, raw_turn):
                raw, parts = w_raw[:, s % RAW_SLOTS, :], w_split[s % WEIGHT_SLOTS]
                pool.wait_ge(raw_in[s % RAW_SLOTS], raw_turn)
                pool.sem_inc(pool_passed, 1)
                pool.tensor_scalar(parts[:, 0, :], raw, 1.0, 1.0, ALU.mult, ALU.mult).then_inc(high_made, 1)
                pool.wait_ge(high_made, u + 1)
                pool.tensor_tensor(parts[:, 1, :], raw, parts[:, 0, :].bitcast(fp32),
                                   ALU.subtract).then_inc(w_ready, 1)

            def residual(t, posted, ready):
                pool.wait_ge(posted, t + 1)
                pool.tensor_tensor(h[:, t, :], h[:, t, :], y[:, t, :], ALU.add).then_inc(ready, 1)

            def split_in_turn(u):
                pool.wait_ge(w_used, u + 1 - WEIGHT_SLOTS)
                split(u, u % WEIGHT_SLOTS, 16 * (u // RAW_SLOTS + 1))

            def split_units(first, last):
                with pool.Fori(first // WEIGHT_SLOTS, last // WEIGHT_SLOTS) as i:
                    for s in range(WEIGHT_SLOTS):
                        pool.wait_ge(w_used, WEIGHT_SLOTS * i + (s + 1 - WEIGHT_SLOTS))
                        split(WEIGHT_SLOTS * i + s, s, 32 * i + 16 * (s // RAW_SLOTS + 1))

            for s in range(WEIGHT_SLOTS):
                split(s, s, 16 * (s // RAW_SLOTS + 1))
            pool.wait_ge(ws_in, 16)
            pool.affine_select(out=ws_raw[:, :, :], in_=ws_raw[:, :, :], compare_op=ALU.is_ge,
                               fill=0.0, base=0, pattern=[[0, GROUPS], [1, CHUNK]],
                               channel_multiplier=-1).then_inc(ws_masked, 1)
            pool.wait_ge(ws_masked, 1)
            pool.tensor_scalar(ws_split[:, 0, :, :], ws_raw[:, :, :], 1.0, 1.0, ALU.mult,
                               ALU.mult).then_inc(ws_high, 1)
            pool.wait_ge(ws_high, 1)
            pool.tensor_tensor(ws_split[:, 1, :, :], ws_raw[:, :, :],
                               ws_split[:, 0, :, :].bitcast(fp32), ALU.subtract).then_inc(ws_ready, 1)

            split_units(WEIGHT_SLOTS, U_FFN)
            for t in range(TT - 2):
                pool.wait_ge(h_in[t], 16)
                residual(t, h_posted, h_ready)
            split_in_turn(U_FFN)
            split_in_turn(U_FFN + 1)
            for t in range(TT - 2, TT):
                pool.wait_ge(h_in[t], 16)
                residual(t, h_posted, h_ready)
            split_in_turn(U_FFN + 2)
            split_in_turn(U_FFN + 3)
            split_units(U_FFN + 4, U_GATE)
            split_in_turn(U_GATE)
            for t in range(TT):
                residual(t, h2_posted, h2_ready)
                if t == 1:
                    split_in_turn(U_GATE + 1)
            for u in range(U_GATE + 2, UNITS):
                split_in_turn(u)

        @block.tensor
        def _(pe):
            def products(bank, pairs, first=True, last=True):
                n = len(pairs)
                for j, (a_high, a_low, b_high, b_low) in enumerate(pairs):
                    nc.tensor.matmul(bank, a_high, b_high, start=first and j == 0, stop=False)
                    nc.tensor.matmul(bank, a_low, b_high, start=False, stop=False)
                    mm = nc.tensor.matmul(bank, a_high, b_low, start=False, stop=last and j == n - 1)
                return mm

            def turn(name, rows, t, slots=4):
                pe.wait_ge(norms[name]["scaled"], t + 1)
                if t >= 2:
                    pe.wait_ge(norms[name]["split"], t - 1)
                for k in range(KT):
                    mm = nc.tensor.transpose(ps[:, 4 + 2 * (t % 2) + k // 4, k % 4 * P:(k % 4 + 1) * P],
                                             rows[:, t % slots, k * P:(k + 1) * P], ident[:, :])
                mm.then_inc(norms[name]["turned"], 1)

            def share(first_unit, u, t, bank):
                slot, tok = w_split[(first_unit + u) % WEIGHT_SLOTS], slice(t * P, (t + 1) * P)
                return products(ps[:, bank, :],
                                [(hn[:, 0, k, tok], hn[:, 1, k, tok],
                                  slot[:, 0, k % 2 * BANK:(k % 2 + 1) * BANK],
                                  slot[:, 1, k % 2 * BANK:(k % 2 + 1) * BANK]) for k in (2 * u, 2 * u + 1)],
                                first=u == 0, last=u == 3)

            def natural(units, first_unit, done, free):
                for u in range(4):
                    pe.wait_ge(w_ready, units + u + 1)
                    for t in range(TT):
                        if u == 0:
                            free(t)
                        mm = share(first_unit, u, t, t)
                        if u == 3 and t < TT - 1:
                            mm.then_inc(done, 1)
                    mm.then_inc(w_used, 1)

            def whole_tile(first_unit, t, bank, done):
                for u in range(4):
                    pe.wait_ge(w_ready, first_unit + u + 1)
                    mm = share(first_unit, u, t, bank)
                mm.then_inc(done, 1)

            def last_tiles(first_unit, tiles, bank_of, done):
                for u in range(4):
                    for t in tiles:
                        mm = share(first_unit, u, t, bank_of(t))
                        if u == 3 and t < TT - 1:
                            mm.then_inc(done, 1)
                    mm.then_inc(w_used, 1)

            def norm_and_chunk(name, rows, first_unit, done, slots=4, turned=0, free=lambda t: None):
                for t in range(TT // 2):
                    upto = min(TT, 2 * t + 3)
                    while turned < upto:
                        turn(name, rows, turned, slots)
                        turned += 1
                    pe.wait_ge(norms[name]["split"], t + 1)
                    free(t)
                    whole_tile(first_unit, t, t, done)
                pe.wait_ge(norms[name]["split"], TT)
                last_tiles(first_unit, range(TT // 2, TT), lambda t: t, done)

            pe.wait_ge(consts_made, 10)
            norm_and_chunk("pre", xn_first, U_GATING, chunk_done)
            with pe.Fori(1, 3) as i:
                natural(U_GATING + 4 * i, U_GATING, chunk_done,
                        lambda t: pe.wait_ge(chunk_out, TT * i + (t + 1 - TT)))

            pe.wait_ge(chunk_out, 2 * TT + 2)
            pe.wait_ge(wf_ready, 1)
            for half in range(2):
                tok = slice(half * BANK, (half + 1) * BANK)
                mm = products(ps[0:HEADS, half, :],
                              [(wf_split[:, 0, k, :], wf_split[:, 1, k, :],
                                hn[:, 0, k, tok], hn[:, 1, k, tok]) for k in range(KT)])
            mm.then_inc(f_done, 1)

            pe.wait_ge(ws_ready, 1)
            pe.wait_ge(vn_ready, TT)
            for g in range(GROUPS):
                if g < 6:
                    pe.wait_ge(chunk_out, 2 * TT + g + 3)
                else:
                    pe.wait_ge(f_logit, 1)
                ch = slice(g * GROUP_DIM, (g + 1) * GROUP_DIM)
                products(ps[:, (g + 2) % 8, :], [(ws_split[:, 0, g, :], ws_split[:, 1, g, :],
                                                  vn[:, 0, :, ch], vn[:, 1, :, ch])]).then_inc(spatial_done, 1)

            def column_tile(slot, bank, done, free):
                for half in range(2):
                    free(half)
                    tok = slice(half * BANK, (half + 1) * BANK)
                    mm = products(ps[:, (bank + half) % 8, :],
                                  [(slot[:, 0, k * P:(k + 1) * P], slot[:, 1, k * P:(k + 1) * P],
                                    hn[:, 0, k, tok], hn[:, 1, k, tok]) for k in range(KT)])
                    mm.then_inc(done if half == 0 else w_used, 1)

            for j in range(4):
                pe.wait_ge(w_ready, U_QK + j + 1)
                column_tile(w_split[j], 2 * j + 2, qk_done, lambda half: pe.wait_ge(spatial_out, 2 * j + half + 1))
            for j in range(4):
                pe.wait_ge(w_ready, U_QK + 4 + j + 1)
                column_tile(w_split[j], 2 * j + 2, qk_done, lambda half: pe.wait_ge(qk_out, 2 * j + half + 1))
            pe.wait_ge(qk_out, 16)

            def scores(turn_, j):
                a, q = TILES[j]
                if q == 0:
                    pe.wait_ge(heads_ready, SPLITS * (2 * turn_ + a) + 3)
                if j >= 2 or not is_first(turn_):
                    pe.wait_ge(scored, N_TILES * turn_ + j - 1)
                for c in range(q // 4 + 1):
                    n = min((q + 1) * P - c * BANK, BANK)
                    wide = max(n, 2 * P)
                    keys = slice(c * BANK, c * BANK + wide)
                    bank = ps[:, 2 * (j % 2) + c, 0:wide]
                    own = c == q // 4
                    nc.tensor.matmul(bank, q2[a][:, q * P:(q + 1) * P], k2[a][:, 0, keys], start=True, stop=False)
                    if own:
                        nc.tensor.matmul(ps[:, 2 * (j % 2) + c, n - P:n], ident_bf[:, :], causal_bf[:, :],
                                         start=False, stop=False)
                    mm = nc.tensor.matmul(bank, q2[a][:, q * P:(q + 1) * P], k2[a][:, 1, keys],
                                          start=False, stop=True)
                mm.then_inc(scores_done, 1)

            def move_probs(turn_, j):
                a, q = TILES[j]
                pe.wait_ge(exped, N_TILES * turn_ + j + 1)
                for part in range(PARTS[j]):
                    n = PART_AT[j] + part
                    if n >= 2 or not is_first(turn_):
                        pe.wait_ge(p_split, N_PARTS * turn_ + n - 1)
                    for kt in range(4 * part, min(q + 1, 4 * part + 4)):
                        mm = nc.tensor.transpose(ps[:, 4 + n % 2, kt % 4 * P:(kt % 4 + 1) * P],
                                                 probs[:, j % 4, kt * P:(kt + 1) * P], ident[:, :])
                    mm.then_inc(p_moved, 1)

            def values(turn_, m):
                a, blk = divmod(m, TT // 2)
                pe.wait_ge(p_split, N_PARTS * turn_ + PART_AT[2 * m + 2])
                if blk == 0:
                    pe.wait_ge(heads_ready, SPLITS * (2 * turn_ + a) + 4)
                if m >= 1 or not is_first(turn_):
                    pe.wait_ge(out_t_made, BLOCKS * turn_ + m)
                last = 2 * blk + 1
                part = p_turned[m % 2]

                def high(kt, q0):
                    return nc.tensor.matmul(ps[:, 6, q0:256], v2[:, kt, a, :, :], part[:, 0, kt, q0:256],
                                            start=kt == last, stop=kt == 0, skip_group_check=True)

                def low(kt, q0):
                    nc.tensor.matmul(ps[0:HEAD_DIM, 6, q0:256], v2[:, kt, a, 0, :], part[:, 1, kt, q0:256],
                                     start=False, stop=False, skip_group_check=True)

                high(last, P)
                low(last, P)
                for kt in reversed(range(last)):
                    low(kt, 0)
                    mm = high(kt, 0)
                mm.then_inc(pv_done, 1)

            def fold_out(turn_, m):
                pe.wait_ge(out_t_made, BLOCKS * turn_ + m + 1)
                if m >= 1 or not is_first(turn_):
                    pe.wait_ge(attended, BLOCKS * turn_ + m)
                for n in range(2):
                    mm = nc.tensor.matmul(ps[:, 7, n * HEAD_DIM:(n + 1) * HEAD_DIM],
                                          out_t[:, n * P:(n + 1) * P], fold[:, :], start=True, stop=True)
                mm.then_inc(folded, 1)

            def pe_steps(turn_, steps):
                for j in range(steps):
                    if j < N_TILES:
                        scores(turn_, j)
                    if at_ := lagged(turn_, j, 2):
                        move_probs(*at_)
                    if (at_ := lagged(turn_, j, 3)) and at_[1] % 2 == 1:
                        values(at_[0], at_[1] // 2)
                    if (at_ := lagged(turn_, j, 4)) and at_[1] % 2 == 1:
                        fold_out(at_[0], at_[1] // 2)

            pairs_of_heads(pe, pe_steps)
            pe.wait_ge(attended, BLOCKS * PAIRS)

            norm_and_chunk("mix", xn_mix, U_MIX, mix_done)
            second = U_MIX + 4
            for t in range(TT - 2):
                if t >= 3:
                    if t == 3:
                        pe.wait_ge(mix_out, TT)
                    turn("ffn", xn_ffn, t - 3)
                pe.wait_ge(mix_out, t + 1 if t < 4 else TT + t - 3)
                whole_tile(second, t, t % 4, mix_done)
            turn("ffn", xn_ffn, TT - 5)
            pe.wait_ge(mix_out, TT + TT - 4)
            last_tiles(second, range(TT - 2, TT), lambda t: t % 4, mix_done)
            turn("ffn", xn_ffn, TT - 4)
            turn("ffn", xn_ffn, TT - 3)

            def half_tile(unit, bank, half, signal):
                tok, slot = slice(half * BANK, (half + 1) * BANK), w_split[unit % WEIGHT_SLOTS]
                products(ps[:, bank + half, :],
                         [(slot[:, 0, k * P:(k + 1) * P], slot[:, 1, k * P:(k + 1) * P],
                           hn[:, 0, k, tok], hn[:, 1, k, tok]) for k in range(KT)]).then_inc(signal, 1)

            pe.wait_ge(norms["ffn"]["split"], TT // 2)
            for n in range(2):
                pe.wait_ge(mix_out, TT + 5 + 2 * n)
                pe.wait_ge(w_ready, U_FFN + n + 1)
                half_tile(U_FFN + n, 2 * n, 0, (a_done, b_done)[n])
            turn("ffn", xn_ffn, TT - 2)
            turn("ffn", xn_ffn, TT - 1)
            pe.wait_ge(norms["ffn"]["split"], TT)
            pe.wait_ge(mix_out, 2 * TT)
            for n in range(2):
                half_tile(U_FFN + n, 2 * n, 1, w_used)

            def inner(unit, slot, done, free):
                pe.wait_ge(w_ready, unit + 1)
                column_tile(w_split[slot % WEIGHT_SLOTS], 0 if done is a_done else 2, done, free)

            def outer(unit, slot, tiles, hid_wait, out_count):
                for o in range(len(tiles)):
                    pe.wait_ge(w_ready, unit + o + 1)
                pe.wait_ge(hid_ready, hid_wait)
                n = 0
                for t in range(TT):
                    tok = slice(t * P, (t + 1) * P)
                    for c in range(2):
                        if out_count is not None or n >= 4:
                            pe.wait_ge(out_added, (0 if out_count is None else out_count) + n - 3)
                        cols = slice(c * BANK, (c + 1) * BANK)
                        mm = products(ps[:, 4 + n % 4, :],
                                      [(hid[s][:, 0, tok], hid[s][:, 1, tok],
                                        w_split[(slot + o) % WEIGHT_SLOTS][:, 0, cols],
                                        w_split[(slot + o) % WEIGHT_SLOTS][:, 1, cols])
                                       for o, s in enumerate(tiles)])
                        n += 1
                        if n < 2 * TT:
                            mm.then_inc(out_done, 1)
                mm.then_inc(w_used, len(tiles))

            def free_a(count):
                return lambda half: pe.wait_ge(a_out, count + half - 1)

            def free_b(count):
                return lambda half: pe.wait_ge(hid_made, count + half - 1)

            inner(U_FFN + 2, 2, a_done, free_a(2))
            outer(U_FFN + 3, 3, [0], 2, None)
            inner(U_FFN + 4, 4, b_done, free_b(2))
            with pe.Fori(0, (FT // 2 - 1) // 2) as i:
                for g in range(2):
                    unit, slot = U_FFN + 5 + 12 * i + 6 * g, 5 + 6 * g
                    hidden = 8 * i + 4 * g
                    inner(unit, slot, a_done, free_a(hidden + 4))
                    inner(unit + 1, slot + 1, b_done, free_b(hidden + 4))
                    inner(unit + 2, slot + 2, a_done, free_a(hidden + 6))
                    outer(unit + 3, slot + 3, [1, 0], hidden + 6, 32 * i + 16 * g + 16)
                    inner(unit + 5, slot + 5, b_done, free_b(hidden + 6))
            outer(U_FFN + 3 * FT - 1, 3 * FT - 1, [1], 2 * FT, 16 * (FT // 2))

            def embedding(t):
                tok = slice(t * P, (t + 1) * P)
                if t >= 2:
                    pe.wait_ge(e_out, t - 1)
                for c in range(2):
                    cols = slice(c * BANK, (c + 1) * BANK)
                    mm = products(ps[:, 2 * (t % 2) + c, :],
                                  [(pt_split[k][:, 0, tok], pt_split[k][:, 1, tok],
                                    w_split[(U_PLE + k) % WEIGHT_SLOTS][:, 0, cols],
                                    w_split[(U_PLE + k) % WEIGHT_SLOTS][:, 1, cols]) for k in range(2)])
                mm.then_inc(*((ple_done, 1) if t < TT - 1 else (w_used, 2)))

            pe.wait_ge(w_ready, U_PLE + 2)
            pe.wait_ge(pt_ready, 2)
            pe.wait_ge(hid_made, 2 * FT)
            embedding(0)
            embedding(1)
            pe.wait_ge(out_added, 16 * (FT // 2 + 1))
            for t in range(2, TT):
                turn("gate", xn_gate, t - 2, 2)
                embedding(t)
            norm_and_chunk("gate", xn_gate, U_GATE, gate_done, slots=2, turned=TT - 2,
                           free=lambda t: pe.wait_ge(e_out, TT - 1 if t < 2 else TT))
            for t in range(TT):
                pe.wait_ge(gate_out, t + 1)
                whole_tile(U_GATE + 4, t, t, gate_done)

        @block.scalar
        def _(act):
            step = Steps(act, act_step)
            act.dma_start(x_tiles[:, 0, :], x[0:P, :]).then_inc(x_in[0], 16)
            act.dma_start(gain[:, 0, :], gains[G_PRE:G_PRE + 1, :].partition_broadcast(P)).then_inc(gain_in, 16)
            for t in range(1, TT):
                act.dma_start(x_tiles[:, t, :], x[t * P:(t + 1) * P, :]).then_inc(x_in[t], 16)
            act.dma_start(ws_raw[:, :, :], ws_t).then_inc(ws_in, 16)
            act.dma_start(gain[:, 1, 0:D_GM], gm_gain.partition_broadcast(P)).then_inc(const_in, 16)
            act.dma_start(bs_col[:, :], b_s).then_inc(const_in, 16)
            act.dma_start(bf_col[0:HEADS, :], b_forget).then_inc(const_in, 16)

            def root(dst, src, scale):
                return act.activation(dst, src, ACT.Sqrt, bias=eps[:, 0:1], scale=scale)

            def statistics(norm, t, squared, rooted, src, scratch):
                act.activation(scratch, src, ACT.Square, accum_out=stat[:, norm, 0, 0, t:t + 1]).then_inc(squared, 1)
                act.wait_ge(squared, t + 1)
                root(stat[:, norm, 1, 0, t:t + 1], stat[:, norm, 0, 0, t:t + 1], SQRT_ALL).then_inc(rooted, 1)

            def evacuate(name, t):
                act.wait_ge(norms[name]["turned"], t + 1)
                for b in range(2):
                    act.activation(hn[:, 0, 4 * b:4 * b + 4, t * P:(t + 1) * P],
                                   ps[:, 4 + 2 * (t % 2) + b, :].rearrange("p (k c) -> p k c", k=4),
                                   ACT.Copy).then_inc(norms[name]["high"], 1)

            act.wait_ge(consts_made, 10)
            for t in range(TT + 2):
                if t < TT:
                    act.wait_ge(x_in[t], 16)
                    statistics(0, t, norms["pre"]["squared"], norms["pre"]["rooted"], x_tiles[:, t, :],
                               junk_first[:, :])
                if t >= 2:
                    evacuate("pre", t - 2)

            act.wait_ge(ws_ready, 1)
            act.dma_start(wf_raw[:, :, :], w_forget).then_inc(wf_in, 16)

            act.wait_ge(norms["pre"]["scaled"], TT)
            for n, dst in enumerate((gv, gu, v_raw)):
                for t in range(TT):
                    chunk_full(act, chunk_done, n, U_GATING, t)
                    act.activation(dst[:, t, :], ps[:, t, :], ACT.Gelu_apprx_tanh if n < 2 else ACT.Copy
                                   ).then_inc(chunk_out, 1)
                if n == 1:
                    act.wait_ge(var_ready, 1)
                    act.activation(g_var[:, :], g_var[:, :], ACT.Sqrt, bias=eps[:, 0:1],
                                   scale=1.0 / GROUP_DIM).then_inc(var_rooted, 1)
                    for t in range(TT):
                        act.wait_ge(vn_scaled, t + 1)
                        act.activation(vn[:, 0, t, :], gv[:, t, :], ACT.Copy).then_inc(vn_high, 1)

            act.wait_ge(f_logit, 1)
            z, e = forget[0:HEADS, 0, :], forget[0:HEADS, 1, :]
            step(act.activation(e, z, ACT.Abs))
            step(act.activation(e, e, ACT.Exp, scale=-1.0))
            act.activation(e, e, ACT.Ln, bias=1.0).then_inc(f_ln, 1)

            act.wait_ge(spatial_done, GROUPS)
            with act.Fori(0, 2) as i:
                for j in range(8):
                    pair, which, half = j // 4, j // 2 % 2, j % 2
                    tile_full(act, qk_done, 4 * i + j // 2, U_QK + 4 * i + j // 2, half)
                    act.activation(qk_raw[:, bass.ds(2 * i + pair, 1), which, half * BANK:(half + 1) * BANK]
                                   .rearrange("p a n -> p (a n)"),
                                   ps[:, (j + 2) % 8, :], ACT.Copy).then_inc(qk_out, 1)

            act.wait_ge(c_ready, 1)
            act.dma_start(c_scratch, forget[0:HEADS, 2, :]).then_inc(c_out, 16)

            def raw(which, turn_, a):
                rows = slice(a * HEAD_DIM, (a + 1) * HEAD_DIM)
                return qk_raw[rows, bass.ds(turn_, 1), which, :].rearrange("p a n -> p (a n)")

            def load_bias(turn_, a):
                act.dma_start(forget_bias[:, a, :],
                              c_scratch[bass.ds(2 * turn_ + a, 1), :].partition_broadcast(P)
                              ).then_inc(bias_in[a], 16)

            def split_head(turn_, a, n):
                own = slice(a * HEAD_DIM, (a + 1) * HEAD_DIM)
                other = slice((1 - a) * HEAD_DIM, (2 - a) * HEAD_DIM)
                if n == 0:
                    dst, src = q2[a][own, :], raw(0, turn_, a)
                elif n < 3:
                    dst, src = k2[a][own if n == 1 else other, 0, :], raw(1, turn_, a)
                else:
                    dst = v2[:, :, a, 0, :]
                    src = v_raw[:, :, bass.ds(turn_ * P + a * HEAD_DIM, HEAD_DIM)]
                act.activation(dst, src, ACT.Copy).then_inc(heads_high, 1)

            def exps(turn_, j):
                a, q = TILES[j]
                n = (q + 1) * P
                act.wait_ge(scored, N_TILES * turn_ + j + 1)
                act.activation(probs[:, j % 4, 0:n], probs[:, j % 4, 0:n], ACT.Exp, scale=-1.0,
                               bias=neg_max[:, j:j + 1], accum_out=row_sum[:, j:j + 1]).then_inc(exped, 1)

            def probs_high(turn_, j):
                a, q = TILES[j]
                m = j // 2
                if j % 2 == 0 and (m >= 2 or not is_first(turn_)):
                    act.wait_ge(pv_done, BLOCKS * turn_ + m - 1)
                for part in range(PARTS[j]):
                    n = PART_AT[j] + part
                    act.wait_ge(p_moved, N_PARTS * turn_ + n + 1)
                    k0, k1 = 4 * part, min(q + 1, 4 * part + 4)
                    act.activation(p_turned[m % 2][:, 0, k0:k1, q % 2 * P:(q % 2 + 1) * P],
                                   ps[:, 4 + n % 2, 0:(k1 - k0) * P].rearrange("p (k c) -> p k c", c=P),
                                   ACT.Copy).then_inc(p_high, 1)

            def out_t_copy(turn_, m):
                act.wait_ge(pv_done, BLOCKS * turn_ + m + 1)
                if m >= 1 or not is_first(turn_):
                    act.wait_ge(folded, BLOCKS * turn_ + m)
                act.activation(out_t[:, :], ps[:, 6, 0:256], ACT.Copy).then_inc(out_t_made, 1)

            def act_steps(turn_, steps):
                last = isinstance(turn_, int) and turn_ == PAIRS - 1
                for j in range(steps):
                    if at_ := lagged(turn_, j, 2):
                        probs_high(*at_)
                    if j < N_TILES:
                        exps(turn_, j)
                    if (at_ := lagged(turn_, j, 3)) and at_[1] % 2 == 1:
                        out_t_copy(at_[0], at_[1] // 2)
                    if j in SPLIT_AT:
                        a, n = SPLIT_AT[j]
                        if a == 1 and n == 0:
                            if not is_first(turn_):
                                act.wait_ge(scores_done, N_TILES * turn_)
                                act.wait_ge(scored, N_TILES * turn_)
                            load_bias(turn_, 1)
                        if a == 1 and n == 3 and not is_first(turn_):
                            act.wait_ge(pv_done, BLOCKS * turn_)
                        if a == 0 and not last and n == 0:
                            act.wait_ge(scored, N_TILES * turn_ + TT)
                            load_bias(turn_ + 1, 0)
                        if a == 0 and not last and n == 3:
                            act.wait_ge(pv_done, BLOCKS * turn_ + BLOCKS // 2)
                        if a == 1 or not last:
                            split_head(turn_ if a == 1 else turn_ + 1, a, n)

            act.wait_ge(c_out, 16)
            load_bias(0, 0)
            for n in range(SPLITS):
                split_head(0, 0, n)
            pairs_of_heads(act, act_steps)
            act.wait_ge(attended, BLOCKS * PAIRS)

            act.dma_start(gain[:, 0, :], gains[G_MIX:G_MIX + 1, :].partition_broadcast(P)).then_inc(gain_in, 16)
            act.dma_start(gain[:, 1, :], gains[G_POST:G_POST + 1, :].partition_broadcast(P)).then_inc(gain_in, 16)
            for t in range(TT + 2):
                if t < TT:
                    tok = slice(t * P, (t + 1) * P)
                    act.activation(junk[:, 0:D_ATT].rearrange("p (a c) -> p a c", a=PAIRS), qk_raw[:, :, 0, tok],
                                   ACT.Square, accum_out=stat[:, 1, 0, 0, t:t + 1]).then_inc(norms["mix"]["squared"], 1)
                    act.activation(junk[:, D_ATT:], gu[:, t, :], ACT.Square,
                                   accum_out=stat[:, 1, 0, 1, t:t + 1]).then_inc(norms["mix"]["squared"], 1)
                    act.wait_ge(norms["mix"]["squared"], 2 * t + 2)
                    root(stat[:, 1, 1, :, t:t + 1], stat[:, 1, 0, :, t:t + 1], SQRT_HALF
                         ).then_inc(norms["mix"]["rooted"], 1)
                if t >= 2:
                    evacuate("mix", t - 2)
            act.wait_ge(norms["mix"]["scaled"], TT)
            act.dma_start(gain[:, 0, :], gains[G_FFN:G_FFN + 1, :].partition_broadcast(P)).then_inc(gain_in, 16)
            for t in range(TT):
                act.dma_start(h[:, t, :], x[t * P:(t + 1) * P, :]).then_inc(h_in[t], 16)

            def mix_evacuate(c, t):
                chunk_full(act, mix_done, c, U_MIX, t)
                act.activation(y[:, t, c * BANK:(c + 1) * BANK], ps[:, t if c == 0 else t % 4, :], ACT.Copy
                               ).then_inc(mix_out, 1)

            def norm_statistics(name, norm, t, ready):
                act.wait_ge(ready, t + 1)
                statistics(norm, t, norms[name]["squared"], norms[name]["rooted"], h[:, t, :], junk[:, :])

            for t in range(TT):
                mix_evacuate(0, t)
            for t in range(TT + 3):
                if t >= 3:
                    evacuate("ffn", t - 3)
                if t < TT:
                    mix_evacuate(1, t)
                    act.wait_ge(mix_out, TT + t + 1)
                    statistics(2, t, post_squared, post_rooted, y[:, t, :], junk[:, :])
                if 1 <= t <= TT:
                    norm_statistics("ffn", 3, t - 1, h_ready)
            act.dma_start(gain[:, 1, :], gains[G_FFN_POST:G_FFN_POST + 1, :].partition_broadcast(P)
                          ).then_inc(gain_in, 16)
            act.dma_start(gain[:, 0, :], gains[G_PLE:G_PLE + 1, :].partition_broadcast(P)).then_inc(gain_in, 16)

            def hidden(tile, unit, first=False):
                for half in range(2):
                    tile_full(act, a_done, tile, unit, half)
                    if not first:
                        act.wait_ge(hid_made, 2 * tile + half - 1)
                    act.activation(silu_a[:, half, :], ps[:, half, :], ACT.Silu).then_inc(a_out, 1)

            def hidden_high(slot, tile, outs):
                if outs is not None:
                    act.wait_ge(w_used, outs)
                for half in range(2):
                    act.wait_ge(hid_made, 2 * tile + half + 1)
                    act.activation(hid[slot][:, 0, half * BANK:(half + 1) * BANK], hid_raw[:, half, :],
                                   ACT.Copy).then_inc(hid_high, 1)

            hidden(0, U_FFN, True)
            hidden_high(0, 0, None)
            hidden(1, U_FFN + 2)
            hidden_high(1, 1, None)
            with act.Fori(0, (FT // 2 - 1) // 2) as i:
                for g in range(2):
                    tile, unit = 4 * i + 2 * g + 2, U_FFN + 5 + 12 * i + 6 * g
                    hidden(tile, unit)
                    hidden_high(0, tile, unit - 1)
                    hidden(tile + 1, unit + 2)
                    hidden_high(1, tile + 1, unit + 5)

            act.wait_ge(w_used, U_PLE - 1)
            act.dma_start(pt_raw[:, :, :], p_t).then_inc(pt_in, 16)
            act.wait_ge(pt_in, 16)
            act.activation(pt_split[0][:, 0, :], pt_raw[:, 0, :], ACT.Copy).then_inc(pt_high, 1)
            act.wait_ge(w_used, U_PLE)
            act.activation(pt_split[1][:, 0, :], pt_raw[:, 1, :], ACT.Copy).then_inc(pt_high, 1)
            for t in range(TT + 3):
                if t < TT:
                    act.wait_ge(out_added, 16 * (FT // 2) + 2 * t + 2)
                    statistics(4, t, ffn_squared, ffn_rooted, y[:, t, :], junk[:, :])
                if 1 <= t <= TT:
                    norm_statistics("gate", 5, t - 1, h2_ready)
                if 2 <= t < TT + 2:
                    n = t - 2
                    act.wait_ge(*((ple_done, n + 1) if n < TT - 1 else (w_used, U_PLE + 2)))
                    banks = ps[:, 2 * (n % 2):2 * (n % 2) + 2, :]
                    act.activation(junk[:, :].rearrange("p (b c) -> p b c", b=2), banks, ACT.Square,
                                   accum_out=stat[:, 6, 0, 0, n:n + 1]).then_inc(e_squared, 1)
                    act.wait_ge(e_squared, n + 1)
                    act.activation(y[:, n, :].rearrange("p (b c) -> p b c", b=2), banks, ACT.Copy
                                   ).then_inc(e_out, 1)
                if t >= 3:
                    evacuate("gate", t - 3)
            root(stat[:, 6, 1, 0, :], stat[:, 6, 0, 0, :], SQRT_ALL).then_inc(e_rooted, 1)

            for n in range(2 * TT):
                c, t = divmod(n, TT)
                if c == 0:
                    chunk_full(act, gate_done, c, U_GATE, t)
                else:
                    act.wait_ge(gate_done, TT - 1 + t + 1)
                    act.wait_ge(row_ready, n - 7)
                act.activation(gates[:, n % 8, :], ps[:, t, :], ACT.Sigmoid).then_inc(gate_out, 1)

        @block.vector
        def _(dve):
            step = Steps(dve, dve_step)

            def low_parts(name, t):
                for b in range(2):
                    dve.wait_ge(norms[name]["high"], 2 * t + b + 1)
                    hi = hn[:, 0, 4 * b:4 * b + 4, t * P:(t + 1) * P].bitcast(fp32)
                    ins = dve.tensor_tensor(hn[:, 1, 4 * b:4 * b + 4, t * P:(t + 1) * P],
                                            ps[:, 4 + 2 * (t % 2) + b, :].rearrange("p (k c) -> p k c", k=4),
                                            hi, ALU.subtract)
                ins.then_inc(norms[name]["split"], 1)

            def inverse(norm, t, halves=1):
                step(dve.reciprocal(stat[:, norm, 2, 0:halves, t:t + 1], stat[:, norm, 1, 0:halves, t:t + 1]))

            def slot_turned(name, t, slots=4):
                if t >= slots:
                    dve.wait_ge(norms[name]["turned"], t + 1 - slots)

            dve.wait_ge(gain_in, 16)
            dve.wait_ge(const_in, 16 * 3)
            for t in range(TT + 2):
                if t < TT:
                    dve.wait_ge(norms["pre"]["rooted"], t + 1)
                    inverse(0, t)
                    slot_turned("pre", t)
                    dve.scalar_tensor_tensor(out=xn_first[:, t % 4, :], in0=x_tiles[:, t, :],
                                             scalar=stat[:, 0, 2, 0, t:t + 1], in1=gain[:, 0, :],
                                             op0=ALU.mult, op1=ALU.mult).then_inc(norms["pre"]["scaled"], 1)
                if t >= 2:
                    low_parts("pre", t - 2)

            for t in range(TT):
                dve.wait_ge(chunk_out, t + 1)
                groups = gv[:, t, :].rearrange("p (g c) -> p g c", g=GROUPS)
                gs = slice(t * GROUPS, (t + 1) * GROUPS)
                step(dve.tensor_reduce(g_sum[:, gs], groups, AX.X, ALU.add))
                step(dve.tensor_scalar(g_sum[:, gs], g_sum[:, gs], -1.0 / GROUP_DIM, None, ALU.mult))
                step(dve.tensor_tensor(groups, groups, g_sum[:, gs].unsqueeze(2).broadcast_to([P, GROUPS, GROUP_DIM]),
                                       ALU.add))
                sq = squares[:, t % 2, :]
                step(dve.tensor_tensor(sq, gv[:, t, :], gv[:, t, :], ALU.mult))
                ins = dve.tensor_reduce(g_var[:, gs], sq.rearrange("p (g c) -> p g c", g=GROUPS), AX.X, ALU.add)
                if t < TT - 1:
                    step(ins)
            ins.then_inc(var_ready, 1)
            dve.wait_ge(wf_in, 16)
            step(dve.tensor_copy(wf_split[:, 0, :, :], wf_raw[:, :, :]))
            dve.tensor_tensor(wf_split[:, 1, :, :], wf_raw[:, :, :], wf_split[:, 0, :, :].bitcast(fp32),
                              ALU.subtract).then_inc(wf_ready, 1)

            dve.wait_ge(var_rooted, 1)
            step(dve.reciprocal(g_inv[:, :], g_var[:, :]))
            for t in range(TT + 1):
                if t < TT:
                    groups = gv[:, t, :].rearrange("p (g c) -> p g c", g=GROUPS)
                    gs = slice(t * GROUPS, (t + 1) * GROUPS)
                    step(dve.tensor_tensor(groups, groups,
                                           g_inv[:, gs].unsqueeze(2).broadcast_to([P, GROUPS, GROUP_DIM]),
                                           ALU.mult))
                    dve.tensor_tensor(gv[:, t, :], gv[:, t, :], gain[:, 1, 0:D_GM], ALU.mult).then_inc(vn_scaled, 1)
                if t >= 1:
                    dve.wait_ge(vn_high, t)
                    dve.tensor_tensor(vn[:, 1, t - 1, :], gv[:, t - 1, :], vn[:, 0, t - 1, :].bitcast(fp32),
                                      ALU.subtract).then_inc(vn_ready, 1)

            z, ln1p, c_row = forget[0:HEADS, 0, :], forget[0:HEADS, 1, :], forget[0:HEADS, 2, :]
            dve.wait_ge(f_done, 1)
            dve.wait_ge(vn_ready, TT)
            dve.tensor_scalar(z.rearrange("p (b c) -> p b c", b=2), ps[0:HEADS, 0:2, :], bf_col[0:HEADS, 0:1], None,
                              ALU.add).then_inc(f_logit, 1)
            dve.wait_ge(f_logit, 1)

            for g in range(GROUPS):
                dve.wait_ge(spatial_done, g + 1)
                ch = slice(g * GROUP_DIM, (g + 1) * GROUP_DIM)
                dve.scalar_tensor_tensor(out=gu[:, :, ch], in0=ps[:, (g + 2) % 8, :].rearrange("p (n c) -> p n c", n=TT),
                                         scalar=bs_col[:, g:g + 1], in1=gu[:, :, ch],
                                         op0=ALU.add, op1=ALU.mult).then_inc(spatial_out, 1)

            dve.wait_ge(f_ln, 1)
            step(dve.scalar_tensor_tensor(out=ln1p, in0=z, scalar=0.0, in1=ln1p, op0=ALU.min, op1=ALU.subtract))
            step(dve.memset(z, 0.0))
            step(dve.tensor_tensor_scan(c_row, ln1p, z, 0.0, ALU.add, ALU.add))
            dve.tensor_scalar(c_row, c_row, -float(HEAD_DIM) ** 0.5, None, ALU.mult).then_inc(c_ready, 1)

            def score(turn_, j):
                a, q = TILES[j]
                n = (q + 1) * P
                if q == 0:
                    dve.wait_ge(bias_in[a], 16 * turn_ + 16)
                if at_ := lagged(turn_, j, 4):
                    dve.wait_ge(p_moved, N_PARTS * at_[0] + PART_AT[at_[1] + 1])
                dve.wait_ge(scores_done, N_TILES * turn_ + j + 1)
                dve.sem_inc(dve_passed, 1)
                src = ps[:, 2 * (j % 2):2 * (j % 2) + 2, :].rearrange("p b c -> p (b c)")[:, 0:n]
                dve.tensor_tensor_reduce(probs[:, j % 4, 0:n], src, forget_bias[:, a, 0:n],
                                         -float(HEAD_DIM) ** -0.5, 3e38, ALU.add, ALU.min,
                                         neg_max[:, j:j + 1]).then_inc(scored, 1)

            def probs_low(turn_, j):
                a, q = TILES[j]
                for part in range(PARTS[j]):
                    n = PART_AT[j] + part
                    dve.wait_ge(p_high, N_PARTS * turn_ + n + 1)
                    k0, k1 = 4 * part, min(q + 1, 4 * part + 4)
                    cols = slice(q % 2 * P, (q % 2 + 1) * P)
                    both = p_turned[j // 2 % 2]
                    dve.tensor_tensor(both[:, 1, k0:k1, cols],
                                      ps[:, 4 + n % 2, 0:(k1 - k0) * P].rearrange("p (k c) -> p k c", c=P),
                                      both[:, 0, k0:k1, cols].bitcast(fp32), ALU.subtract).then_inc(p_split, 1)

            def attend(turn_, m):
                a, blk = divmod(m, TT // 2)
                dve.wait_ge(exped, N_TILES * turn_ + 2 * m + 2)
                step(dve.reciprocal(row_inv[:, 2 * m:2 * m + 2], row_sum[:, 2 * m:2 * m + 2]))
                dve.wait_ge(folded, BLOCKS * turn_ + m + 1)
                for n in range(2):
                    t = 2 * blk + n
                    col = t * P + a * HEAD_DIM
                    ins = dve.tensor_scalar(qk_raw[:, bass.ds(turn_, 1), 0, col:col + HEAD_DIM].rearrange("p a n -> p (a n)"),
                                            ps[:, 7, n * HEAD_DIM:(n + 1) * HEAD_DIM],
                                            row_inv[:, 2 * m + n:2 * m + n + 1], None, ALU.mult)
                ins.then_inc(attended, 1)

            def raw(which, turn_, a):
                rows = slice(a * HEAD_DIM, (a + 1) * HEAD_DIM)
                return qk_raw[rows, bass.ds(turn_, 1), which, :].rearrange("p a n -> p (a n)")

            def split_head(turn_, a, n):
                own = slice(a * HEAD_DIM, (a + 1) * HEAD_DIM)
                other = slice((1 - a) * HEAD_DIM, (2 - a) * HEAD_DIM)
                if n == 0:
                    dst, src, hi = q2[a][other, :], raw(0, turn_, a), q2[a][own, :]
                elif n < 3:
                    dst, src, hi = k2[a][own if n == 1 else other, 1, :], raw(1, turn_, a), k2[a][own, 0, :]
                else:
                    dst, hi = v2[:, :, a, 1, :], v2[:, :, a, 0, :]
                    src = v_raw[:, :, bass.ds(turn_ * P + a * HEAD_DIM, HEAD_DIM)]
                dve.wait_ge(heads_high, SPLITS * (2 * turn_ + a) + n + 1)
                dve.tensor_tensor(dst, src, hi.bitcast(fp32), ALU.subtract).then_inc(heads_ready, 1)

            def dve_steps(turn_, steps):
                last = isinstance(turn_, int) and turn_ == PAIRS - 1
                if not isinstance(turn_, int):
                    step.loop(turn_ - 1, BLOCKS)
                for j in range(steps):
                    if j < N_TILES:
                        score(turn_, j)
                    if at_ := lagged(turn_, j, 2):
                        probs_low(*at_)
                    if j in SPLIT_AT:
                        a, n = SPLIT_AT[j]
                        if a == 1:
                            split_head(turn_, a, n)
                        elif not last:
                            split_head(turn_ + 1, a, n)
                    if (at_ := lagged(turn_, j, 4)) and at_[1] % 2 == 1:
                        attend(at_[0], at_[1] // 2)
                if not isinstance(turn_, int):
                    step.end_loop(PAIRS - 2)

            for n in range(SPLITS):
                split_head(0, 0, n)
            pairs_of_heads(dve, dve_steps)
            dve.wait_ge(attended, BLOCKS * PAIRS)

            dve.wait_ge(gain_in, 48)
            for t in range(TT + 2):
                if t < TT:
                    dve.wait_ge(norms["mix"]["rooted"], t + 1)
                    inverse(1, t, 2)
                    slot_turned("mix", t)
                    tok = slice(t * P, (t + 1) * P)
                    for half, src in enumerate((qk_raw[:, :, 0, tok], gu[:, t, :])):
                        cols = slice(half * D_ATT, (half + 1) * D_ATT)
                        dst, g = xn_mix[:, t % 4, cols], gain[:, 0, cols]
                        if half == 0:
                            dst = dst.rearrange("p (a c) -> p a c", a=PAIRS)
                            g = g.rearrange("p (a c) -> p a c", a=PAIRS)
                        ins = dve.scalar_tensor_tensor(out=dst, in0=src, scalar=stat[:, 1, 2, half, t:t + 1],
                                                       in1=g, op0=ALU.mult, op1=ALU.mult)
                    ins.then_inc(norms["mix"]["scaled"], 1)
                if t >= 2:
                    low_parts("mix", t - 2)

            def post(norm, t, rooted, posted):
                dve.wait_ge(rooted, t + 1)
                inverse(norm, t)
                dve.scalar_tensor_tensor(out=y[:, t, :], in0=y[:, t, :], scalar=stat[:, norm, 2, 0, t:t + 1],
                                         in1=gain[:, 1, :], op0=ALU.mult, op1=ALU.mult).then_inc(posted, 1)

            for t in range(TT + 3):
                if t >= 3:
                    low_parts("ffn", t - 3)
                if t < TT:
                    post(2, t, post_rooted, h_posted)
                if 1 <= t <= TT:
                    n = t - 1
                    if t == 1:
                        dve.wait_ge(gain_in, 64)
                    dve.wait_ge(norms["ffn"]["rooted"], n + 1)
                    inverse(3, n)
                    slot_turned("ffn", n)
                    dve.scalar_tensor_tensor(out=xn_ffn[:, n % 4, :], in0=h[:, n, :], scalar=stat[:, 3, 2, 0, n:n + 1],
                                             in1=gain[:, 0, :], op0=ALU.mult, op1=ALU.mult
                                             ).then_inc(norms["ffn"]["scaled"], 1)

            def hidden(slot, tile, unit):
                for half in range(2):
                    cols = slice(half * BANK, (half + 1) * BANK)
                    tile_full(dve, b_done, tile, unit, half)
                    dve.wait_ge(a_out, 2 * tile + half + 1)
                    dve.tensor_tensor(hid_raw[:, half, :], ps[:, 2 + half, :], silu_a[:, half, :],
                                      ALU.mult).then_inc(hid_made, 1)
                for half in range(2):
                    cols = slice(half * BANK, (half + 1) * BANK)
                    dve.wait_ge(hid_high, 2 * tile + half + 1)
                    dve.tensor_tensor(hid[slot][:, 1, cols], hid_raw[:, half, :],
                                      hid[slot][:, 0, cols].bitcast(fp32), ALU.subtract).then_inc(hid_ready, 1)
                dve.wait_ge(hid_ready, 2 * tile + 2)

            def add_out(turn_, last_unit, copy=False):
                for n in range(2 * TT):
                    t, cols = n // 2, slice(n % 2 * BANK, (n % 2 + 1) * BANK)
                    if n < 2 * TT - 1:
                        dve.wait_ge(out_done, (2 * TT - 1) * turn_ + n + 1)
                    else:
                        dve.wait_ge(w_used, last_unit + 1)
                    if copy:
                        if n == 0:
                            dve.wait_ge(h_ready, TT)
                        dve.tensor_copy(y[:, t, cols], ps[:, 4 + n % 4, :]).then_inc(out_added, 1)
                    else:
                        dve.tensor_tensor(y[:, t, cols], ps[:, 4 + n % 4, :], y[:, t, cols],
                                          ALU.add).then_inc(out_added, 1)
                    if isinstance(turn_, int) and turn_ == FT // 2 and n == 11:
                        embedding_low(0)

            def embedding_low(k):
                dve.wait_ge(pt_high, k + 1)
                dve.tensor_tensor(pt_split[k][:, 1, :], pt_raw[:, k, :], pt_split[k][:, 0, :].bitcast(fp32),
                                  ALU.subtract).then_inc(pt_ready, 1)

            hidden(0, 0, U_FFN + 1)
            add_out(0, U_FFN + 3, copy=True)
            hidden(1, 1, U_FFN + 4)
            with dve.Fori(0, (FT // 2 - 1) // 2) as i:
                for g in range(2):
                    tile, unit = 4 * i + 2 * g + 2, U_FFN + 5 + 12 * i + 6 * g
                    hidden(0, tile, unit + 1)
                    dve.wait_ge(out_added, 32 * i + 16 * g + 16)
                    add_out(2 * i + g + 1, unit + 4)
                    hidden(1, tile + 1, unit + 5)
            dve.wait_ge(out_added, 16 * (FT // 2))
            add_out(FT // 2, U_FFN + 3 * FT - 1)

            embedding_low(1)
            dve.wait_ge(gain_in, 96)
            for t in range(TT + 3):
                if t < TT:
                    post(4, t, ffn_rooted, h2_posted)
                if 1 <= t <= TT:
                    n = t - 1
                    dve.wait_ge(norms["gate"]["rooted"], n + 1)
                    inverse(5, n)
                    slot_turned("gate", n, 2)
                    dve.tensor_scalar(xn_gate[:, n % 2, :], h[:, n, :], stat[:, 5, 2, 0, n:n + 1], None, ALU.mult
                                      ).then_inc(norms["gate"]["scaled"], 1)
                if t >= 3:
                    low_parts("gate", t - 3)

            dve.wait_ge(e_rooted, 1)
            step(dve.reciprocal(stat[:, 6, 2, 0, :], stat[:, 6, 1, 0, :]))
            for t in range(TT):
                dve.wait_ge(e_out, t + 1)
                dve.scalar_tensor_tensor(out=y[:, t, :], in0=y[:, t, :], scalar=stat[:, 6, 2, 0, t:t + 1],
                                         in1=gain[:, 0, :], op0=ALU.mult, op1=ALU.mult).then_inc(e_scaled, 1)
            for n in range(2 * TT):
                t, cols = n % TT, slice(n // TT * BANK, (n // TT + 1) * BANK)
                dve.wait_ge(e_scaled, t + 1)
                dve.wait_ge(gate_out, n + 1)
                step(dve.tensor_tensor(gates[:, n % 8, :], gates[:, n % 8, :], y[:, t, cols], ALU.mult))
                dve.tensor_tensor(h[:, t, cols], h[:, t, cols], gates[:, n % 8, :], ALU.add).then_inc(row_ready, 1)


def kernel(x, p, mix_pre_norm, mix_post_norm, w_in, b_forget, gm_v_norm, gm_w_s, gm_b_s, mix_out_norm,
           w_out, ffn_pre_norm, ffn_post_norm, w_ffn_in, w_ffn_out, w_ple, ple_norm, w_ple_gate):
    import concourse.bacc as bacc
    from concourse.bass_utils import run_bass_kernel_spmd

    f = lambda a: np.asarray(a)
    w_in, w_out, w_ffn_in, w_ffn_out, w_ple, w_gate = (
        f(a)[0] for a in (w_in, w_out, w_ffn_in, w_ffn_out, w_ple, w_ple_gate))

    def chunk(w):
        return w.reshape(-1, 2, P, BANK).transpose(0, 2, 1, 3).reshape(-1, P, UNIT)

    def columns(w):
        return w.reshape(1, KT, P, P).transpose(0, 2, 1, 3).reshape(1, P, UNIT)

    q0, k0, v0 = 0, D_ATT, 2 * D_ATT
    f0 = 3 * D_ATT
    g0 = f0 + HEADS
    units = [chunk(w_in[:, g0 + D_GM:]), chunk(w_in[:, g0:g0 + D_GM]), chunk(w_in[:, v0:v0 + D_ATT])]
    for pair in range(PAIRS):
        units += [columns(w_in[:, c + pair * P:c + (pair + 1) * P]) for c in (q0, k0)]
    units += [chunk(w_out[:, :BANK]), chunk(w_out[:, BANK:])]
    a = [columns(w_ffn_in[:, j * P:(j + 1) * P]) for j in range(FT)]
    b = [columns(w_ffn_in[:, D_FF + j * P:D_FF + (j + 1) * P]) for j in range(FT)]
    o = [w_ffn_out[None, j * P:(j + 1) * P, :] for j in range(FT)]
    for j in range(0, FT, 2):
        units += [a[j], b[j], a[j + 1], *o[max(j - 1, 0):j + 1], b[j + 1]]
    units += [o[FT - 1], w_ple.reshape(2, P, UNIT), chunk(w_gate[:, :BANK]), chunk(w_gate[:, BANK:])]
    packed = np.concatenate(units, axis=0)
    assert packed.shape[0] == UNITS

    arrays = {
        "x": f(x)[0],
        "weights": packed,
        "w_forget": w_in[:, f0:g0].reshape(KT, P, HEADS).transpose(1, 0, 2),
        "b_forget": f(b_forget)[0][:, None],
        "p_t": f(p)[0, 0].T.reshape(2, P, TOKENS).transpose(1, 0, 2),
        "ws_t": f(gm_w_s)[0].transpose(2, 0, 1),
        "b_s": f(gm_b_s)[0].T,
        "gains": np.stack([f(g)[0] for g in (mix_pre_norm, mix_out_norm, mix_post_norm, ffn_pre_norm,
                                             ffn_post_norm, ple_norm)]),
        "gm_gain": f(gm_v_norm),
    }
    nc = bacc.Bacc("TRN2", target_bir_lowering=False, num_devices=1)
    fp32 = mybir.dt.float32
    aps = {}
    for name, value in arrays.items():
        arrays[name] = value = np.ascontiguousarray(value)
        aps[name] = nc.dram_tensor(name, value.shape, mybir.dt.from_np(value.dtype), kind="ExternalInput").ap()
    c_scratch = nc.dram_tensor("c_scratch", (HEADS, TOKENS), fp32).ap()
    out = nc.dram_tensor("out", (TOKENS, D_MODEL), fp32, kind="ExternalOutput").ap()
    build_trunk(nc, c_scratch=c_scratch, out=out, **aps)
    result = run_bass_kernel_spmd(nc, [arrays], core_ids=[0])
    return result.results[0]["out"].reshape(1, TOKENS, D_MODEL)
```

```python
import concourse.bass as bass
import numpy as np
from concourse import mybir

TOKENS, D_MODEL = 1024, 1024
HEADS, HEAD_DIM = 8, 64
D_ATT = HEADS * HEAD_DIM
GROUPS, GROUP_DIM, CHUNK = 8, 64, 128
D_GM = GROUPS * GROUP_DIM
D_FF = ((8 * D_MODEL // 3 + 255) // 256) * 256
PLE_DIM = 256
EPS = 1e-6

P = 128
TT = TOKENS // P
KT = D_MODEL // P
FT = D_FF // P
PAIRS = HEADS // 2
BANK = 512
UNIT = 1024
NT_COLS = D_MODEL // P

U_GATING, U_QK, U_MIX = 0, 12, 20
U_FFN = U_MIX + 8
U_LAST = U_FFN + 3 * FT - 2
U_PLE = U_FFN + 3 * FT
U_GATE = U_PLE + 2
UNITS = U_GATE + 8
RAW_SLOTS, WEIGHT_SLOTS = 2, 4
WARM_UP = 36


class Steps:

    def __init__(self, engine, semaphore):
        self.engine, self.semaphore, self.done, self.turn = engine, semaphore, 0, 0

    def __call__(self, instruction):
        instruction.then_inc(self.semaphore, 1)
        self.done += 1
        self.engine.wait_ge(self.semaphore, self.turn + self.done)

    def loop(self, i, per):
        self.start, self.per, self.turn = self.done, per, i * per

    def end_loop(self, turns):
        assert self.done - self.start == self.per
        self.done, self.turn = self.start + turns * self.per, 0


def build_trunk(nc, x, weights, w_forget, b_forget, p_t, ws_t, b_s, gains, gm_gain, c_scratch, out):
    fp32, fp32r, bf16 = mybir.dt.float32, mybir.dt.float32r, mybir.dt.bfloat16
    ALU, ACT, AX = mybir.AluOpType, mybir.ActivationFunctionType, mybir.AxisListType

    KB = 1024
    base = (nc.sbuf_base + 63) // 64 * 64
    at = {"ring": base, "raw": base + 32 * KB, "gain": base + 40 * KB, "hn": base + 48 * KB,
          "f": base + 112 * KB, "small": base + 204 * KB}

    def place(name, shape, dtype, region, kb=0.0):
        return nc.alloc_sbuf_tensor_at(name, [P, *shape], dtype, offset=at[region] + int(kb * KB))

    w_raw = place("w_raw", [RAW_SLOTS, UNIT], fp32, "raw")
    w_split = [place(f"w_split{s}", [2, UNIT], fp32r, "ring", 8 * s) for s in range(WEIGHT_SLOTS)]
    gain = place("gain", [2, D_MODEL], fp32, "gain")
    hn = place("hn", [2, KT, TOKENS], fp32r, "hn")

    x_tiles = place("x_tiles", [TT, D_MODEL], fp32, "f", 0)
    xn_first = place("xn_first", [4, D_MODEL], fp32, "f", 48)
    gv = place("gv", [TT, D_GM], fp32, "f", 0)
    gu = place("gu", [TT, D_GM], fp32, "f", 16)
    v_raw = place("v_raw", [TT, D_ATT], fp32, "f", 32)
    vn = place("vn", [2, TT, D_GM], fp32r, "f", 48)
    qk_raw = place("qk_raw", [PAIRS, 2, TOKENS], fp32, "f", 48)
    junk_first = place("junk_first", [D_MODEL], bf16, "f", 32)
    w_first = place("w_first", [2, UNIT], fp32, "f", 36)
    squares = place("squares", [2, D_GM], fp32, "f", 48)
    ws_split = place("ws_split", [2, GROUPS, CHUNK], fp32r, "f", 80)
    ws_raw = place("ws_raw", [GROUPS, CHUNK], fp32, "f", 88)

    p_turned = [place(f"p_turned{s}", [2, TT, 256], fp32r, "hn", 16 * s) for s in range(2)]
    q2 = [place(f"q2_{a}", [TOKENS], fp32r, "f", 12 * a) for a in range(2)]
    k2 = [place("k2_0", [2, TOKENS], fp32r, "f", 4), place("k2_1", [2, TOKENS], fp32r, "hn", 48)]
    v2 = place("v2", [TT, 2, 2, HEAD_DIM], fp32r, "hn", 56)
    probs = place("probs", [4, TOKENS], fp32, "hn", 32)
    forget_bias = place("forget_bias", [2, TOKENS], fp32, "f", 80)
    out_t = place("out_t", [256], fp32, "f", 88)
    forget = place("forget", [3, TOKENS], fp32, "f", 0)
    wf_raw = place("wf_raw", [KT, HEADS], fp32, "f", 89)
    wf_split = place("wf_split", [2, KT, HEADS], fp32r, "f", 89.5)

    junk_mix = place("junk_mix", [2, D_ATT], bf16, "f", 90)
    xn_mix = place("xn_mix", [4, D_MODEL], fp32, "f", 0)
    y = place("y", [TT, D_MODEL], fp32, "f", 0)
    h = place("h", [TT, D_MODEL], fp32, "f", 32)
    xn_ffn = place("xn_ffn", [4, D_MODEL], fp32, "f", 64)
    junk = place("junk", [D_MODEL], bf16, "f", 88)
    hid = [place(f"hid{s}", [2, TOKENS], fp32r, "f", 64 + 8 * s) for s in range(2)]
    silu_a = place("silu_a", [2, BANK], fp32, "f", 80)
    hid_raw = place("hid_raw", [2, BANK], fp32, "f", 84)
    pt_raw = place("pt_raw", [2, TOKENS], fp32, "f", 80)
    pt_tile = [place("pt_tile0", [2, 2, P], fp32r, "f", 90), place("pt_tile1", [2, 2, P], fp32r, "gain", 0)]
    gates = place("gates", [8, BANK], fp32, "f", 64)

    ident = place("ident", [P], fp32, "small", 0)
    ident_bf = place("ident_bf", [P], bf16, "small", 0.5)
    causal_bf = place("causal_bf", [P], bf16, "small", 0.75)
    fold = place("fold", [HEAD_DIM], fp32, "small", 1)
    bs_col = place("bs_col", [GROUPS], fp32, "small", 1.25)
    bf_col = place("bf_col", [1], fp32, "small", 1.3125)
    row_sum = place("row_sum", [2 * TT], fp32, "small", 1.375)
    row_inv = place("row_inv", [2 * TT], fp32, "small", 1.5)
    neg_max = place("neg_max", [2 * TT], fp32, "small", 1.625)
    g_sum = place("g_sum", [TT * GROUPS], fp32, "small", 1.75)
    g_var = place("g_var", [TT * GROUPS], fp32, "small", 2)
    g_inv = place("g_inv", [TT * GROUPS], fp32, "small", 2.25)
    stat = place("stat", [7, 3, 2, TT], fp32, "small", 2.5)
    eps = place("eps", [1], fp32, "small", 3.8125)
    ps = nc.alloc_psum_tensor("ps", [P, 8, BANK], fp32)

    def sem(name):
        return nc.alloc_semaphore(name)

    first_in = [sem(f"first_in{n}") for n in range(2)]
    first_high, first_ready = sem("first_high"), sem("first_ready")
    second_ready = sem("second_ready")
    raw_in = [sem(f"raw_in{s}") for s in range(RAW_SLOTS)]
    high_made, w_ready, w_used = sem("high_made"), sem("w_ready"), sem("w_used")
    x_in = [sem(f"x_in{t}") for t in range(TT)]
    h_in = [sem(f"h_in{t}") for t in range(TT)]
    const_in, ws_in, pt_in, gain_in = sem("const_in"), sem("ws_in"), sem("pt_in"), sem("gain_in")
    pool_passed, dve_passed = sem("pool_passed"), sem("dve_passed")
    consts_made, wf_in, wf_ready = sem("consts_made"), sem("wf_in"), sem("wf_ready")
    ws_masked, ws_high, ws_ready = sem("ws_masked"), sem("ws_high"), sem("ws_ready")
    dve_step, act_step = sem("dve_step"), sem("act_step")
    norms = {n: {k: sem(f"norm_{n}_{k}") for k in ("squared", "rooted", "scaled", "turned", "high", "split")}
             for n in ("pre", "mix", "ffn", "gate")}
    chunk_done, chunk_out = sem("chunk_done"), sem("chunk_out")
    var_ready, var_rooted, vn_scaled, vn_high, vn_ready = (
        sem("var_ready"), sem("var_rooted"), sem("vn_scaled"), sem("vn_high"), sem("vn_ready"))
    spatial_done, spatial_out = sem("spatial_done"), sem("spatial_out")
    qk_done, qk_out, f_done, f_logit, f_exp, f_ln, c_ready, c_out = (
        sem("qk_done"), sem("qk_out"), sem("f_done"), sem("f_logit"), sem("f_exp"), sem("f_ln"),
        sem("c_ready"), sem("c_out"))
    bias_in = [sem(f"bias_in{a}") for a in range(2)]
    heads_high, heads_ready = sem("heads_high"), sem("heads_ready")
    scores_done, scored, exped, p_moved, p_high, p_split = (
        sem("scores_done"), sem("scored"), sem("exped"), sem("p_moved"), sem("p_high"), sem("p_split"))
    pv_done, out_t_made, folded, attended = sem("pv_done"), sem("out_t_made"), sem("folded"), sem("attended")
    mix_done, mix_out = sem("mix_done"), sem("mix_out")
    post_squared, post_rooted, h_ready = sem("post_squared"), sem("post_rooted"), sem("h_ready")
    a_done, a_out, b_done, hid_made, hid_high, hid_ready, out_done, out_added = (
        sem("a_done"), sem("a_out"), sem("b_done"), sem("hid_made"), sem("hid_high"),
        sem("hid_ready"), sem("out_done"), sem("out_added"))
    ffn_squared, ffn_rooted, h2_ready = sem("ffn_squared"), sem("ffn_rooted"), sem("h2_ready")
    h_posted, h2_posted, h_late = sem("h_posted"), sem("h2_posted"), sem("h_late")
    gate_inverted = sem("gate_inverted")
    gate_done, gate_out, pt_high, pt_ready = sem("gate_done"), sem("gate_out"), sem("pt_high"), sem("pt_ready")
    ple_done, e_out, e_squared, e_rooted, e_scaled, row_ready, stored = (
        sem("ple_done"), sem("e_out"), sem("e_squared"), sem("e_rooted"), sem("e_scaled"),
        sem("row_ready"), sem("stored"))

    first_units = [(0, w_raw[:, 0, :], raw_in[0]), (2, w_first[:, 0, :], first_in[0]),
                   (3, w_first[:, 1, :], first_in[1])]
    G_PRE, G_MIX, G_POST, G_FFN, G_FFN_POST, G_PLE = range(6)
    SQRT_ALL, SQRT_HALF = 1.0 / D_MODEL, 1.0 / D_ATT

    TILES = [(a, q) for a in range(2) for q in range(TT)]
    PARTS = [q // 4 + 1 for _, q in TILES]
    PART_AT = [sum(PARTS[:j]) for j in range(len(TILES) + 1)]
    BLOCKS = len(TILES) // 2
    N_TILES, N_PARTS = len(TILES), PART_AT[-1]
    MIX_TILES_AT = {N_TILES - 2: (0, 1), N_TILES + 1: (2, 3), N_TILES + 4: range(4, TT)}
    DEPTH = 5
    SPLITS = 4

    def gate_bank(t):
        return 2 if t < TT - 1 else 0

    def h_signal(t):
        return (h_ready, t + 1) if t < TT - 2 else (h_late, t + 3 - TT)

    def lagged(turn, j, lag):
        if j >= lag:
            return (turn, j - lag) if j - lag < N_TILES else None
        return None if is_first(turn) else (turn - 1, j - lag + N_TILES)

    def is_first(turn):
        return isinstance(turn, int) and turn == 0

    def head_operand(turn_, a, n):
        own = slice(a * HEAD_DIM, (a + 1) * HEAD_DIM)
        other = slice((1 - a) * HEAD_DIM, (2 - a) * HEAD_DIM)
        if n == 0:
            return q2[a][own, :], q2[a][other, :], head_raw(0, turn_, a), q2[a][own, :]
        if n < 3:
            rows = own if n == 1 else other
            return k2[a][rows, 0, :], k2[a][rows, 1, :], head_raw(1, turn_, a), k2[a][own, 0, :]
        return (v2[:, :, a, 0, :], v2[:, :, a, 1, :],
                v_raw[:, :, bass.ds(turn_ * P + a * HEAD_DIM, HEAD_DIM)], v2[:, :, a, 0, :])

    def head_raw(which, turn_, a):
        rows = slice(a * HEAD_DIM, (a + 1) * HEAD_DIM)
        return qk_raw[rows, bass.ds(turn_, 1), which, :].rearrange("p a n -> p (a n)")

    def pairs_of_heads(engine, body):
        body(0, N_TILES)
        with engine.Fori(1, PAIRS - 1) as i:
            body(i, N_TILES)
        body(PAIRS - 1, N_TILES + DEPTH)

    def chunk_full(engine, done, chunk, first_unit, t):
        if t < TT - 1:
            engine.wait_ge(done, (TT - 1) * chunk + t + 1)
        else:
            engine.wait_ge(w_used, first_unit + 4 * chunk + 4)

    def tile_full(engine, done, tiles, unit, half):
        if half == 0:
            engine.wait_ge(done, tiles + 1)
        else:
            engine.wait_ge(w_used, unit + 1)

    block = nc.Block()
    with block:

        @block.sync
        def _(sp):
            def load_x(t):
                sp.dma_start(x_tiles[:, t, :], x[t * P:(t + 1) * P, :]).then_inc(x_in[t], 16)

            load_x(0)
            for s in range(RAW_SLOTS):
                sp.dma_start(w_raw[:, s, :], weights[s]).then_inc(raw_in[s], 16)
            for n in range(2):
                sp.dma_start(w_first[:, n, :], weights[RAW_SLOTS + n]).then_inc(first_in[n], 16)
            for t in range(1, TT):
                load_x(t)
            with sp.Fori(2, UNITS // RAW_SLOTS) as i:
                for s in range(RAW_SLOTS):
                    sp.wait_ge(w_ready, RAW_SLOTS * i + (s + 1 - RAW_SLOTS))
                    sp.dma_start(w_raw[:, s, :], weights[bass.ds(RAW_SLOTS * i + s, 1)][0]
                                 ).then_inc(raw_in[s], 16)
            for n in range(2 * TT):
                t, cols = n % TT, slice(n // TT * BANK, (n // TT + 1) * BANK)
                sp.wait_ge(row_ready, n + 1)
                sp.dma_start(out[t * P:(t + 1) * P, cols], h[:, t, cols]).then_inc(stored, 16)
            sp.wait_ge(stored, 16 * 2 * TT)

        @block.gpsimd
        def _(pool):
            pool.memset(ident[:, :], 0.0).then_inc(consts_made, 1)
            pool.memset(ident_bf[:, :], 0.0).then_inc(consts_made, 1)
            pool.memset(causal_bf[:, :], 0.0).then_inc(consts_made, 1)
            pool.memset(fold[:, :], 0.0).then_inc(consts_made, 1)
            pool.memset(eps[:, :], EPS).then_inc(consts_made, 1)
            pool.wait_ge(consts_made, 5)
            for m in (ident, ident_bf):
                pool.affine_select(out=m[:, :], in_=m[:, :], compare_op=ALU.not_equal, fill=1.0, base=0,
                                   pattern=[[-1, P]], channel_multiplier=1).then_inc(consts_made, 1)
            pool.affine_select(out=causal_bf[:, :], in_=causal_bf[:, :], compare_op=ALU.is_ge, fill=-1e30,
                               base=0, pattern=[[-1, P]], channel_multiplier=1).then_inc(consts_made, 1)
            for half in range(2):
                pool.wait_ge(consts_made, 8 + half)
                pool.affine_select(out=fold[:, :], in_=fold[:, :], compare_op=ALU.not_equal, fill=1.0,
                                   base=-HEAD_DIM * half, pattern=[[-1, HEAD_DIM]],
                                   channel_multiplier=1).then_inc(consts_made, 1)

            def split(u, s, raw_turn, ready=w_ready):
                raw, parts = w_raw[:, s % RAW_SLOTS, :], w_split[s % WEIGHT_SLOTS]
                pool.wait_ge(raw_in[s % RAW_SLOTS], raw_turn)
                pool.sem_inc(pool_passed, 1)
                pool.tensor_scalar(parts[:, 0, :], raw, 1.0, 1.0, ALU.mult, ALU.mult).then_inc(high_made, 1)
                pool.wait_ge(high_made, 1 if ready is second_ready else u - 2)
                pool.tensor_tensor(parts[:, 1, :], raw, parts[:, 0, :].bitcast(fp32),
                                   ALU.subtract).then_inc(ready, 1)

            def residual(t, posted, ready):
                pool.wait_ge(posted, t + 1)
                pool.tensor_tensor(h[:, t, :], h[:, t, :], y[:, t, :], ALU.add).then_inc(ready, 1)

            def split_in_turn(u):
                pool.wait_ge(w_used, u + 1 - WEIGHT_SLOTS)
                split(u, u % WEIGHT_SLOTS, 16 * (u // RAW_SLOTS))

            def split_units(first, last):
                with pool.Fori(first // WEIGHT_SLOTS, last // WEIGHT_SLOTS) as i:
                    for s in range(WEIGHT_SLOTS):
                        pool.wait_ge(w_used, WEIGHT_SLOTS * i + (s + 1 - WEIGHT_SLOTS))
                        split(WEIGHT_SLOTS * i + s, s, 32 * i + 16 * (s // RAW_SLOTS))

            split(1, 1, 16, second_ready)
            pool.wait_ge(second_ready, 1)
            pool.wait_ge(first_ready, 3)
            pool.sem_inc(w_ready, WEIGHT_SLOTS)
            pool.wait_ge(ws_in, 16)
            pool.affine_select(out=ws_raw[:, :, :], in_=ws_raw[:, :, :], compare_op=ALU.is_ge,
                               fill=0.0, base=0, pattern=[[0, GROUPS], [1, CHUNK]],
                               channel_multiplier=-1).then_inc(ws_masked, 1)
            pool.wait_ge(ws_masked, 1)
            pool.tensor_scalar(ws_split[:, 0, :, :], ws_raw[:, :, :], 1.0, 1.0, ALU.mult,
                               ALU.mult).then_inc(ws_high, 1)
            pool.wait_ge(ws_high, 1)
            pool.tensor_tensor(ws_split[:, 1, :, :], ws_raw[:, :, :],
                               ws_split[:, 0, :, :].bitcast(fp32), ALU.subtract).then_inc(ws_ready, 1)

            split_units(WEIGHT_SLOTS, U_MIX + WEIGHT_SLOTS)

            def split_head(turn_, a):
                for n in range(SPLITS):
                    high, low, src, near = head_operand(turn_, a, n)
                    if turn_ > 0 and n == 0:
                        pool.wait_ge(scores_done, N_TILES * (turn_ - 1) + (a + 1) * TT)
                    if turn_ > 0 and n == 3:
                        pool.wait_ge(pv_done, BLOCKS * (turn_ - 1) + (a + 1) * TT // 2)
                    pool.wait_ge(heads_ready, SPLITS * (2 * turn_ + a) + n)
                    pool.tensor_scalar(high, src, 1.0, 1.0, ALU.mult, ALU.mult).then_inc(heads_high, 1)
                    pool.wait_ge(heads_high, SPLITS * (2 * turn_ + a) + n + 1)
                    pool.tensor_tensor(low, src, near.bitcast(fp32), ALU.subtract).then_inc(heads_ready, 1)

            pool.wait_ge(qk_out, 4 * PAIRS)
            pool.wait_ge(w_ready, U_MIX + WEIGHT_SLOTS)
            for head in range(1, HEADS):
                split_head(head // 2, head % 2)
            pool.wait_ge(heads_ready, SPLITS * HEADS)
            split_units(U_MIX + WEIGHT_SLOTS, U_FFN)
            for t in range(TT - 2):
                pool.wait_ge(h_in[t], 16)
                residual(t, h_posted, h_ready)
            for u in range(U_FFN, U_FFN + WEIGHT_SLOTS):
                split_in_turn(u)
            split_units(U_FFN + 4, U_GATE)
            for t in range(TT - 1):
                residual(t, h2_posted, h2_ready)
            split_in_turn(U_GATE)
            split_in_turn(U_GATE + 1)
            residual(TT - 1, h2_posted, h2_ready)
            for u in range(U_GATE + 2, UNITS):
                split_in_turn(u)

        @block.tensor
        def _(pe):
            def products(bank, pairs, first=True, last=True):
                n = len(pairs)
                for j, (a_high, a_low, b_high, b_low) in enumerate(pairs):
                    nc.tensor.matmul(bank, a_high, b_high, start=first and j == 0, stop=False)
                    nc.tensor.matmul(bank, a_low, b_high, start=False, stop=False)
                    mm = nc.tensor.matmul(bank, a_high, b_low, start=False, stop=last and j == n - 1)
                return mm

            def turn(name, rows, t, slots=4):
                pe.wait_ge(norms[name]["scaled"], t + 1)
                if t >= 2:
                    pe.wait_ge(norms[name]["split"], t - 1)
                for k in range(KT):
                    mm = nc.tensor.transpose(ps[:, 4 + 2 * (t % 2) + k // 4, k % 4 * P:(k % 4 + 1) * P],
                                             rows[:, t % slots, k * P:(k + 1) * P], ident[:, :])
                mm.then_inc(norms[name]["turned"], 1)

            def share(first_unit, u, t, bank):
                slot, tok = w_split[(first_unit + u) % WEIGHT_SLOTS], slice(t * P, (t + 1) * P)
                return products(ps[:, bank, :],
                                [(hn[:, 0, k, tok], hn[:, 1, k, tok],
                                  slot[:, 0, k % 2 * BANK:(k % 2 + 1) * BANK],
                                  slot[:, 1, k % 2 * BANK:(k % 2 + 1) * BANK]) for k in (2 * u, 2 * u + 1)],
                                first=u == 0, last=u == 3)

            def natural(units, first_unit, done, free):
                for u in range(4):
                    pe.wait_ge(w_ready, units + u + 1)
                    for t in range(TT):
                        if u == 0:
                            free(t)
                        mm = share(first_unit, u, t, t)
                        if u == 3 and t < TT - 1:
                            mm.then_inc(done, 1)
                    mm.then_inc(w_used, 1)

            def whole_tile(first_unit, t, bank, done, between=lambda: None):
                for u in range(4):
                    if first_unit == 0:
                        pe.wait_ge(*((second_ready, 1) if u == 1 else (first_ready, max(1, u))))
                    else:
                        pe.wait_ge(w_ready, first_unit + u + 1)
                    mm = share(first_unit, u, t, bank)
                    if u == 2:
                        between()
                mm.then_inc(done, 1)

            def last_tiles(first_unit, tiles, bank_of, done):
                for u in range(4):
                    for t in tiles:
                        mm = share(first_unit, u, t, bank_of(t))
                        if u == 3 and t < TT - 1:
                            mm.then_inc(done, 1)
                    mm.then_inc(w_used, 1)

            def norm_and_chunk(name, rows, first_unit, done, slots=4, turned=0, free=lambda t: None,
                               order=(2, 4, 6, 8)):
                def turn_upto(n):
                    nonlocal turned
                    for t in range(turned, n):
                        turn(name, rows, t, slots)
                    turned = max(turned, n)

                for t in range(TT // 2):
                    turn_upto(order[t])
                    pe.wait_ge(norms[name]["split"], t + 1)
                    free(t)
                    whole_tile(first_unit, t, t, done, lambda: turn_upto(min(TT, turned + 1)))
                pe.wait_ge(norms[name]["split"], TT)
                last_tiles(first_unit, range(TT // 2, TT), lambda t: t, done)

            pe.wait_ge(consts_made, 10)
            for _ in range(WARM_UP):
                nc.tensor.matmul(ps[:, 0, 0:P], ident_bf[:, :], ident_bf[:, :], start=True, stop=True)
            norm_and_chunk("pre", xn_first, U_GATING, chunk_done, order=(1, 3, 5, 7))
            with pe.Fori(1, 3) as i:
                natural(U_GATING + 4 * i, U_GATING, chunk_done,
                        lambda t: pe.wait_ge(chunk_out, TT * i + (t + 1 - TT)))

            pe.wait_ge(chunk_out, 2 * TT + 2)
            pe.wait_ge(wf_ready, 1)
            for half in range(2):
                tok = slice(half * BANK, (half + 1) * BANK)
                mm = products(ps[0:HEADS, half, :],
                              [(wf_split[:, 0, k, :], wf_split[:, 1, k, :],
                                hn[:, 0, k, tok], hn[:, 1, k, tok]) for k in range(KT)])
            mm.then_inc(f_done, 1)

            pe.wait_ge(ws_ready, 1)
            pe.wait_ge(vn_ready, TT)
            for g in range(GROUPS):
                if g < 6:
                    pe.wait_ge(chunk_out, 2 * TT + g + 3)
                else:
                    pe.wait_ge(f_logit, 1)
                ch = slice(g * GROUP_DIM, (g + 1) * GROUP_DIM)
                products(ps[:, (g + 2) % 8, :], [(ws_split[:, 0, g, :], ws_split[:, 1, g, :],
                                                  vn[:, 0, :, ch], vn[:, 1, :, ch])]).then_inc(spatial_done, 1)

            def column_tile(slot, bank, done, free):
                for half in range(2):
                    free(half)
                    tok = slice(half * BANK, (half + 1) * BANK)
                    mm = products(ps[:, (bank + half) % 8, :],
                                  [(slot[:, 0, k * P:(k + 1) * P], slot[:, 1, k * P:(k + 1) * P],
                                    hn[:, 0, k, tok], hn[:, 1, k, tok]) for k in range(KT)])
                    mm.then_inc(done if half == 0 else w_used, 1)

            for j in range(4):
                pe.wait_ge(w_ready, U_QK + j + 1)
                column_tile(w_split[j], 2 * j + 2, qk_done, lambda half: pe.wait_ge(spatial_out, 2 * j + half + 1))
            for j in range(4):
                pe.wait_ge(w_ready, U_QK + 4 + j + 1)
                column_tile(w_split[j], 2 * j + 2, qk_done, lambda half: pe.wait_ge(qk_out, 2 * j + half + 1))
            pe.wait_ge(qk_out, 16)

            def scores(turn_, j):
                a, q = TILES[j]
                if q == 0:
                    pe.wait_ge(heads_ready, SPLITS * (2 * turn_ + a) + 3)
                if j >= 2 or not is_first(turn_):
                    pe.wait_ge(scored, N_TILES * turn_ + j - 1)
                for c in range(q // 4 + 1):
                    n = min((q + 1) * P - c * BANK, BANK)
                    wide = max(n, 2 * P)
                    keys = slice(c * BANK, c * BANK + wide)
                    bank = ps[:, 2 * (j % 2) + c, 0:wide]
                    own = c == q // 4
                    nc.tensor.matmul(bank, q2[a][:, q * P:(q + 1) * P], k2[a][:, 0, keys], start=True, stop=False)
                    if own:
                        nc.tensor.matmul(ps[:, 2 * (j % 2) + c, n - P:n], ident_bf[:, :], causal_bf[:, :],
                                         start=False, stop=False)
                    mm = nc.tensor.matmul(bank, q2[a][:, q * P:(q + 1) * P], k2[a][:, 1, keys],
                                          start=False, stop=True)
                mm.then_inc(scores_done, 1)

            def move_probs(turn_, j):
                a, q = TILES[j]
                pe.wait_ge(exped, N_TILES * turn_ + j + 1)
                for part in range(PARTS[j]):
                    n = PART_AT[j] + part
                    if n >= 2 or not is_first(turn_):
                        pe.wait_ge(p_split, N_PARTS * turn_ + n - 1)
                    for kt in range(4 * part, min(q + 1, 4 * part + 4)):
                        mm = nc.tensor.transpose(ps[:, 4 + n % 2, kt % 4 * P:(kt % 4 + 1) * P],
                                                 probs[:, j % 4, kt * P:(kt + 1) * P], ident[:, :])
                    mm.then_inc(p_moved, 1)

            def values(turn_, m):
                a, blk = divmod(m, TT // 2)
                pe.wait_ge(p_split, N_PARTS * turn_ + PART_AT[2 * m + 2])
                if blk == 0:
                    pe.wait_ge(heads_ready, SPLITS * (2 * turn_ + a) + 4)
                if m >= 1 or not is_first(turn_):
                    pe.wait_ge(out_t_made, BLOCKS * turn_ + m)
                last = 2 * blk + 1
                part = p_turned[m % 2]

                def high(kt, q0):
                    return nc.tensor.matmul(ps[:, 6, q0:256], v2[:, kt, a, :, :], part[:, 0, kt, q0:256],
                                            start=kt == last, stop=kt == 0, skip_group_check=True)

                def low(kt, q0):
                    nc.tensor.matmul(ps[0:HEAD_DIM, 6, q0:256], v2[:, kt, a, 0, :], part[:, 1, kt, q0:256],
                                     start=False, stop=False, skip_group_check=True)

                high(last, P)
                low(last, P)
                for kt in reversed(range(last)):
                    low(kt, 0)
                    mm = high(kt, 0)
                mm.then_inc(pv_done, 1)

            def fold_out(turn_, m):
                pe.wait_ge(out_t_made, BLOCKS * turn_ + m + 1)
                if m >= 1 or not is_first(turn_):
                    pe.wait_ge(attended, BLOCKS * turn_ + m)
                for n in range(2):
                    mm = nc.tensor.matmul(ps[:, 7, n * HEAD_DIM:(n + 1) * HEAD_DIM],
                                          out_t[:, n * P:(n + 1) * P], fold[:, :], start=True, stop=True)
                mm.then_inc(folded, 1)

            def pe_steps(turn_, steps):
                for j in range(steps):
                    if j < N_TILES:
                        scores(turn_, j)
                    if at_ := lagged(turn_, j, 2):
                        move_probs(*at_)
                    if (at_ := lagged(turn_, j, 3)) and at_[1] % 2 == 1:
                        values(at_[0], at_[1] // 2)
                    if j == N_TILES + 3:
                        turn("mix", xn_mix, 0)
                    if (at_ := lagged(turn_, j, 4)) and at_[1] % 2 == 1:
                        fold_out(at_[0], at_[1] // 2)

            pairs_of_heads(pe, pe_steps)
            pe.wait_ge(attended, BLOCKS * PAIRS)

            norm_and_chunk("mix", xn_mix, U_MIX, mix_done, turned=1)
            second = U_MIX + 4
            for t in range(TT - 2):
                if t >= 3:
                    if t == 3:
                        pe.wait_ge(mix_out, TT)
                    turn("ffn", xn_ffn, t - 3)
                pe.wait_ge(mix_out, t + 1 if t < 4 else TT + t - 3)
                whole_tile(second, t, t % 4, mix_done)
            turn("ffn", xn_ffn, TT - 5)
            pe.wait_ge(mix_out, TT + TT - 4)
            last_tiles(second, range(TT - 2, TT), lambda t: t % 4, mix_done)
            turn("ffn", xn_ffn, TT - 4)

            def half_tile(unit, bank, half, signal, between=lambda k: None):
                tok, slot = slice(half * BANK, (half + 1) * BANK), w_split[unit % WEIGHT_SLOTS]
                for k in range(KT):
                    mm = products(ps[:, bank + half, :],
                                  [(slot[:, 0, k * P:(k + 1) * P], slot[:, 1, k * P:(k + 1) * P],
                                    hn[:, 0, k, tok], hn[:, 1, k, tok])], first=k == 0, last=k == KT - 1)
                    between(k)
                mm.then_inc(signal, 1)

            def last_turns(k):
                if k in (3, 6):
                    turn("ffn", xn_ffn, TT - 2 if k == 3 else TT - 1)

            pe.wait_ge(norms["ffn"]["split"], TT // 2)
            for n in range(2):
                pe.wait_ge(mix_out, TT + 5 + 2 * n)
                pe.wait_ge(w_ready, U_FFN + n + 1)
                if n == 1:
                    turn("ffn", xn_ffn, TT - 3)
                half_tile(U_FFN + n, 2 * n, 0, (a_done, b_done)[n], (lambda k: None, last_turns)[n])
            pe.wait_ge(norms["ffn"]["split"], TT)
            pe.wait_ge(mix_out, 2 * TT)
            for n in range(2):
                half_tile(U_FFN + n, 2 * n, 1, w_used)

            def inner(unit, slot, done, halves):
                pe.wait_ge(w_ready, unit + 1)
                emptied = a_out if done is a_done else hid_made
                column_tile(w_split[slot % WEIGHT_SLOTS], 0 if done is a_done else 2, done,
                            lambda half: pe.wait_ge(emptied, halves + half - 1))

            def outer(t, unit_slot, added):
                tok = slice(t * P, (t + 1) * P)
                for c in range(2):
                    n, cols = 2 * t + c, slice(c * BANK, (c + 1) * BANK)
                    pe.wait_ge(out_added, added + n)
                    mm = products(ps[:, 4 + n % 4, :],
                                  [(hid[o][:, 0, tok], hid[o][:, 1, tok],
                                    w_split[(unit_slot + o) % WEIGHT_SLOTS][:, 0, cols],
                                    w_split[(unit_slot + o) % WEIGHT_SLOTS][:, 1, cols]) for o in range(2)])
                    mm.then_inc(*((out_done, 1) if n < 2 * TT - 1 else (w_used, 2)))

            inner(U_FFN + 2, 2, a_done, 2)
            inner(U_FFN + 3, 3, b_done, 2)
            with pe.Fori(0, (FT // 2 - 1) // 2) as i:
                for g in range(2):
                    unit, slot = U_FFN + 4 + 12 * i + 6 * g, 6 * g
                    halves = 8 * i + 4 * g + 4
                    inner(unit, slot, a_done, halves)
                    inner(unit + 1, slot + 1, b_done, halves)
                    pe.wait_ge(w_ready, unit + 4)
                    pe.wait_ge(hid_ready, halves)
                    for t in range(TT):
                        outer(t, slot + 2, 32 * i + 16 * g + TT - 3)
                    inner(unit + 4, slot + 4, a_done, halves + 2)
                    inner(unit + 5, slot + 5, b_done, halves + 2)

            def embedding(t, bank):
                pe.wait_ge(pt_ready, t + 1)
                for c in range(2):
                    cols = slice(c * BANK, (c + 1) * BANK)
                    mm = products(ps[:, bank + c, :],
                                  [(pt_tile[t % 2][:, k, 0, :], pt_tile[t % 2][:, k, 1, :],
                                    w_split[(U_PLE + k) % WEIGHT_SLOTS][:, 0, cols],
                                    w_split[(U_PLE + k) % WEIGHT_SLOTS][:, 1, cols]) for k in range(2)])
                mm.then_inc(*((ple_done, 1) if t < TT - 1 else (w_used, 2)))

            def turn_h(t):
                pe.wait_ge(h2_ready, t + 1)
                if 1 <= t < TT - 1:
                    pe.wait_ge(norms["gate"]["split"], t)
                for k in range(KT):
                    mm = nc.tensor.transpose(ps[:, gate_bank(t) + k // 4, k % 4 * P:(k % 4 + 1) * P],
                                             h[:, t, k * P:(k + 1) * P], ident[:, :])
                mm.then_inc(norms["gate"]["turned"], 1)

            last_added = 2 * TT * (FT // 2 - 1) + TT - 3
            pe.wait_ge(w_ready, U_LAST + 2)
            pe.wait_ge(hid_ready, 2 * FT)
            for t in range(TT):
                outer(t, U_LAST, last_added)
                if t >= 2:
                    if t == 2:
                        pe.wait_ge(w_ready, U_PLE + 2)
                        pe.wait_ge(a_out, 2 * FT)
                        pe.wait_ge(hid_made, 2 * FT)
                    else:
                        pe.wait_ge(e_out, t - 2)
                    embedding(t - 2, 0)
                    turn_h(t - 2)
            for t, bank in ((TT - 2, 4), (TT - 1, 6)):
                pe.wait_ge(out_added, last_added + 3 + 2 * t + 2)
                embedding(t, bank)
            turn_h(TT - 2)
            pe.wait_ge(e_out, TT - 2)
            turn_h(TT - 1)

            for t in range(TT // 2):
                pe.wait_ge(norms["gate"]["split"], t + 1)
                pe.wait_ge(e_out, TT - 1 + t // 2)
                whole_tile(U_GATE, t, 4 + t, gate_done)
            pe.wait_ge(norms["gate"]["split"], TT)
            last_tiles(U_GATE, range(TT // 2, TT), lambda t: (t + 4) % 8, gate_done)
            for t in range(TT):
                pe.wait_ge(gate_out, t + 1)
                whole_tile(U_GATE + 4, t, (t + 4) % 8, gate_done)

        @block.scalar
        def _(act):
            step = Steps(act, act_step)
            act.dma_start(gain[:, 0, :], gains[G_PRE:G_PRE + 1, :].partition_broadcast(P)).then_inc(gain_in, 16)

            def root(dst, src, scale):
                return act.activation(dst, src, ACT.Sqrt, bias=eps[:, 0:1], scale=scale)

            def statistics(norm, t, squared, rooted, src, scratch):
                act.activation(scratch, src, ACT.Square, accum_out=stat[:, norm, 0, 0, t:t + 1]).then_inc(squared, 1)
                act.wait_ge(squared, t + 1)
                root(stat[:, norm, 1, 0, t:t + 1], stat[:, norm, 0, 0, t:t + 1], SQRT_ALL).then_inc(rooted, 1)

            def evacuate(name, t, bank=None):
                bank = 4 + 2 * (t % 2) if bank is None else bank
                act.wait_ge(norms[name]["turned"], t + 1)
                for b in range(2):
                    act.activation(hn[:, 0, 4 * b:4 * b + 4, t * P:(t + 1) * P],
                                   ps[:, bank + b, :].rearrange("p (k c) -> p k c", k=4),
                                   ACT.Copy).then_inc(norms[name]["high"], 1)

            act.wait_ge(consts_made, 10)
            step(root(stat[:, 0, 1, 0, 0:1], eps[:, 0:1], 1.0))
            for t in range(TT + 1):
                if t < TT:
                    act.wait_ge(x_in[t], 16)
                    statistics(0, t, norms["pre"]["squared"], norms["pre"]["rooted"], x_tiles[:, t, :],
                               junk_first[:, :])
                if t >= 2:
                    evacuate("pre", t - 1)
                if t == 0:
                    for n, (slot, src, loaded) in enumerate(first_units):
                        act.wait_ge(loaded, 16)
                        act.activation(w_split[slot][:, 0, :], src, ACT.Copy).then_inc(first_high, 1)
                        if n == 0:
                            evacuate("pre", 0)
                if t == 3:
                    act.dma_start(ws_raw[:, :, :], ws_t).then_inc(ws_in, 16)
                    act.dma_start(gain[:, 1, 0:D_GM], gm_gain.partition_broadcast(P)).then_inc(const_in, 16)
                    act.dma_start(bs_col[:, :], b_s).then_inc(const_in, 16)
                    act.dma_start(bf_col[0:HEADS, :], b_forget).then_inc(const_in, 16)

            act.wait_ge(ws_ready, 1)
            act.dma_start(wf_raw[:, :, :], w_forget).then_inc(wf_in, 16)

            act.wait_ge(norms["pre"]["scaled"], TT)
            for n, dst in enumerate((gv, gu, v_raw)):
                for t in range(TT):
                    chunk_full(act, chunk_done, n, U_GATING, t)
                    act.activation(dst[:, t, :], ps[:, t, :], ACT.Gelu_apprx_tanh if n < 2 else ACT.Copy
                                   ).then_inc(chunk_out, 1)
                if n == 1:
                    act.wait_ge(var_ready, 1)
                    act.activation(g_var[:, :], g_var[:, :], ACT.Sqrt, bias=eps[:, 0:1],
                                   scale=1.0 / GROUP_DIM).then_inc(var_rooted, 1)
                    for t in range(TT):
                        act.wait_ge(vn_scaled, t + 1)
                        act.activation(vn[:, 0, t, :], gv[:, t, :], ACT.Copy).then_inc(vn_high, 1)

            act.wait_ge(f_logit, 1)
            z, e = forget[0:HEADS, 0, :], forget[0:HEADS, 1, :]
            step(act.activation(e, z, ACT.Abs))
            step(act.activation(e, e, ACT.Exp, scale=-1.0))
            act.activation(e, e, ACT.Ln, bias=1.0).then_inc(f_ln, 1)

            act.dma_start(gain[:, 0, :], gains[G_MIX:G_MIX + 1, :].partition_broadcast(P)).then_inc(gain_in, 16)
            act.dma_start(gain[:, 1, :], gains[G_POST:G_POST + 1, :].partition_broadcast(P)).then_inc(gain_in, 16)

            def load_bias(turn_, a):
                act.dma_start(forget_bias[:, a, :],
                              c_scratch[bass.ds(2 * turn_ + a, 1), :].partition_broadcast(P)
                              ).then_inc(bias_in[a], 16)

            def first_head(n):
                high, low, src, near = head_operand(0, 0, n)
                act.activation(high, src, ACT.Copy).then_inc(heads_high, 1)

            act.wait_ge(spatial_done, GROUPS)
            for j in range(4 * PAIRS):
                pair, which, half = j // 4, j // 2 % 2, j % 2
                tile_full(act, qk_done, j // 2, U_QK + j // 2, half)
                act.activation(qk_raw[:, pair, which, half * BANK:(half + 1) * BANK], ps[:, (j + 2) % 8, :],
                               ACT.Copy).then_inc(qk_out, 1)
                if j == 3:
                    act.wait_ge(c_ready, 1)
                    act.dma_start(c_scratch, forget[0:HEADS, 2, :]).then_inc(c_out, 16)
                if j == 7:
                    act.wait_ge(c_out, 16)
                    load_bias(0, 0)
                    act.wait_ge(qk_out, 4)
                    for n in range(SPLITS - 1):
                        first_head(n)
            first_head(SPLITS - 1)

            def exps(turn_, j):
                a, q = TILES[j]
                n = (q + 1) * P
                act.wait_ge(scored, N_TILES * turn_ + j + 1)
                act.activation(probs[:, j % 4, 0:n], probs[:, j % 4, 0:n], ACT.Exp, scale=-1.0,
                               bias=neg_max[:, j:j + 1], accum_out=row_sum[:, j:j + 1]).then_inc(exped, 1)

            def probs_high(turn_, j):
                a, q = TILES[j]
                m = j // 2
                if j % 2 == 0 and (m >= 2 or not is_first(turn_)):
                    act.wait_ge(pv_done, BLOCKS * turn_ + m - 1)
                for part in range(PARTS[j]):
                    n = PART_AT[j] + part
                    act.wait_ge(p_moved, N_PARTS * turn_ + n + 1)
                    k0, k1 = 4 * part, min(q + 1, 4 * part + 4)
                    act.activation(p_turned[m % 2][:, 0, k0:k1, q % 2 * P:(q % 2 + 1) * P],
                                   ps[:, 4 + n % 2, 0:(k1 - k0) * P].rearrange("p (k c) -> p k c", c=P),
                                   ACT.Copy).then_inc(p_high, 1)

            def out_t_copy(turn_, m):
                act.wait_ge(pv_done, BLOCKS * turn_ + m + 1)
                if m >= 1 or not is_first(turn_):
                    act.wait_ge(folded, BLOCKS * turn_ + m)
                act.activation(out_t[:, :], ps[:, 6, 0:256], ACT.Copy).then_inc(out_t_made, 1)

            squares_made = 0

            def mix_squares(half, t):
                nonlocal squares_made
                if squares_made >= 2:
                    act.wait_ge(norms["mix"]["squared"], squares_made - 1)
                scratch = junk_mix[:, squares_made % 2, :]
                if half == 0:
                    ins = act.activation(scratch.rearrange("p (a c) -> p a c", a=PAIRS),
                                         qk_raw[:, :, 0, t * P:(t + 1) * P], ACT.Square,
                                         accum_out=stat[:, 1, 0, 0, t:t + 1])
                else:
                    ins = act.activation(scratch, gu[:, t, :], ACT.Square, accum_out=stat[:, 1, 0, 1, t:t + 1])
                ins.then_inc(norms["mix"]["squared"], 1)
                squares_made += 1

            def mix_roots(first, end):
                act.wait_ge(norms["mix"]["squared"], squares_made)
                root(stat[:, 1, 1, :, first:end], stat[:, 1, 0, :, first:end], SQRT_HALF
                     ).then_inc(norms["mix"]["rooted"], end - first)

            def act_steps(turn_, steps):
                last = isinstance(turn_, int) and turn_ == PAIRS - 1
                for j in range(steps):
                    if at_ := lagged(turn_, j, 2):
                        probs_high(*at_)
                    if j < N_TILES:
                        exps(turn_, j)
                    if (at_ := lagged(turn_, j, 3)) and at_[1] % 2 == 1:
                        out_t_copy(at_[0], at_[1] // 2)
                    if last and 6 <= j < 6 + TT:
                        mix_squares(1, j - 6)
                    for t in MIX_TILES_AT.get(j, ()) if last else ():
                        if t % 2 == 0:
                            act.wait_ge(attended, BLOCKS * turn_ + BLOCKS // 2 + t // 2 + 1)
                        mix_squares(0, t)
                    if j == N_TILES + 1:
                        mix_roots(0, 4)
                    if j == N_TILES + 3:
                        evacuate("mix", 0)
                    if j == 1:
                        if not is_first(turn_):
                            act.wait_ge(scored, N_TILES * turn_)
                        load_bias(turn_, 1)
                    if j == TT + 1 and not last:
                        act.wait_ge(scored, N_TILES * turn_ + TT)
                        load_bias(turn_ + 1, 0)

            pairs_of_heads(act, act_steps)
            mix_roots(4, TT)
            for t in range(1, TT):
                evacuate("mix", t)
            act.wait_ge(norms["mix"]["scaled"], TT)
            act.dma_start(gain[:, 0, :], gains[G_FFN:G_FFN + 1, :].partition_broadcast(P)).then_inc(gain_in, 16)
            for t in range(TT):
                act.dma_start(h[:, t, :], x[t * P:(t + 1) * P, :]).then_inc(h_in[t], 16)

            def mix_evacuate(c, t):
                chunk_full(act, mix_done, c, U_MIX, t)
                act.activation(y[:, t, c * BANK:(c + 1) * BANK], ps[:, t if c == 0 else t % 4, :], ACT.Copy
                               ).then_inc(mix_out, 1)

            for t in range(TT):
                mix_evacuate(0, t)
            for t in range(TT + 3):
                if t >= 3:
                    evacuate("ffn", t - 3)
                if t < TT:
                    mix_evacuate(1, t)
                    act.wait_ge(mix_out, TT + t + 1)
                    statistics(2, t, post_squared, post_rooted, y[:, t, :], junk[:, :])
                if 1 <= t <= TT:
                    act.wait_ge(*h_signal(t - 1))
                    statistics(3, t - 1, norms["ffn"]["squared"], norms["ffn"]["rooted"], h[:, t - 1, :],
                               junk[:, :])
            act.dma_start(gain[:, 1, :], gains[G_FFN_POST:G_FFN_POST + 1, :].partition_broadcast(P)
                          ).then_inc(gain_in, 16)

            def hidden(tile, unit, first=False):
                for half in range(2):
                    tile_full(act, a_done, tile, unit, half)
                    if not first:
                        act.wait_ge(hid_made, 2 * tile + half - 1)
                    act.activation(silu_a[:, half, :], ps[:, half, :], ACT.Silu).then_inc(a_out, 1)

            def hidden_high(slot, tile, outs):
                if outs is not None:
                    act.wait_ge(w_used, outs)
                for half in range(2):
                    act.wait_ge(hid_made, 2 * tile + half + 1)
                    act.activation(hid[slot][:, 0, half * BANK:(half + 1) * BANK], hid_raw[:, half, :],
                                   ACT.Copy).then_inc(hid_high, 1)

            hidden(0, U_FFN, True)
            hidden_high(0, 0, None)
            hidden(1, U_FFN + 2)
            hidden_high(1, 1, None)
            with act.Fori(0, (FT // 2 - 1) // 2) as i:
                for g in range(2):
                    tile, unit = 4 * i + 2 * g + 2, U_FFN + 4 + 12 * i + 6 * g
                    hidden(tile, unit)
                    hidden_high(0, tile, unit + 4)
                    hidden(tile + 1, unit + 4)
                    hidden_high(1, tile + 1, unit + 4)

            act.wait_ge(hid_ready, 2 * FT)
            act.dma_start(pt_raw[:, :, :], p_t).then_inc(pt_in, 16)

            def embedding_squares(t, bank):
                act.wait_ge(*((ple_done, t + 1) if t < TT - 1 else (w_used, U_PLE + 2)))
                act.wait_ge(norms["gate"]["squared"], min(t + 2, TT))
                if t == TT - 1:
                    act.wait_ge(e_squared, t)
                act.activation(junk[:, :].rearrange("p (b c) -> p b c", b=2), ps[:, bank:bank + 2, :], ACT.Square,
                               accum_out=stat[:, 6, 0, 0, t:t + 1]).then_inc(e_squared, 1)

            for t in range(TT + 1):
                if t >= 3:
                    evacuate("gate", t - 3, gate_bank(t - 3))
                if t < TT:
                    act.wait_ge(out_added, 2 * TT * (FT // 2 - 1) + TT + 2 * t + 2)
                    if t >= 3:
                        act.wait_ge(e_squared, t - 2)
                    elif t == 2:
                        act.wait_ge(norms["gate"]["squared"], 1)
                    statistics(4, t, ffn_squared, ffn_rooted, y[:, t, :], junk[:, :])
                if t >= 1:
                    act.wait_ge(h2_ready, t)
                    if t == TT:
                        act.wait_ge(e_squared, TT - 2)
                    act.activation(junk[:, :], h[:, t - 1, :], ACT.Square, accum_out=stat[:, 5, 0, 0, t - 1:t]
                                   ).then_inc(norms["gate"]["squared"], 1)
                if t >= 2:
                    embedding_squares(t - 2, 0 if t < TT else 4)
                if t < TT:
                    if t == 0:
                        act.wait_ge(pt_in, 16)
                    act.activation(pt_tile[t % 2][:, :, 0, :], pt_raw[:, :, t * P:(t + 1) * P], ACT.Copy
                                   ).then_inc(pt_high, 1)
            embedding_squares(TT - 1, 6)
            act.dma_start(gain[:, 0, :], gains[G_PLE:G_PLE + 1, :].partition_broadcast(P)).then_inc(gain_in, 16)
            for t in range(TT - 2, TT):
                evacuate("gate", t, gate_bank(t))
            act.wait_ge(norms["gate"]["squared"], TT)
            root(stat[:, 5, 1, 0, :], stat[:, 5, 0, 0, :], SQRT_ALL).then_inc(norms["gate"]["rooted"], 1)
            act.wait_ge(e_squared, TT)
            root(stat[:, 6, 1, 0, :], stat[:, 6, 0, 0, :], SQRT_ALL).then_inc(e_rooted, 1)

            act.wait_ge(gate_inverted, 1)
            for n in range(2 * TT):
                c, t = divmod(n, TT)
                if c == 0:
                    chunk_full(act, gate_done, c, U_GATE, t)
                else:
                    act.wait_ge(gate_done, TT - 1 + t + 1)
                    act.wait_ge(row_ready, n - 7)
                act.activation(gates[:, n % 8, :], ps[:, (t + 4) % 8, :], ACT.Sigmoid,
                               scale=stat[:, 5, 2, 0, t:t + 1]).then_inc(gate_out, 1)

        @block.vector
        def _(dve):
            step = Steps(dve, dve_step)

            def low_parts(name, t, bank=None):
                bank = 4 + 2 * (t % 2) if bank is None else bank
                for b in range(2):
                    dve.wait_ge(norms[name]["high"], 2 * t + b + 1)
                    hi = hn[:, 0, 4 * b:4 * b + 4, t * P:(t + 1) * P].bitcast(fp32)
                    ins = dve.tensor_tensor(hn[:, 1, 4 * b:4 * b + 4, t * P:(t + 1) * P],
                                            ps[:, bank + b, :].rearrange("p (k c) -> p k c", k=4),
                                            hi, ALU.subtract)
                ins.then_inc(norms[name]["split"], 1)

            def inverse(norm, t, halves=1):
                step(dve.reciprocal(stat[:, norm, 2, 0:halves, t:t + 1], stat[:, norm, 1, 0:halves, t:t + 1]))

            def slot_turned(name, t, slots=4):
                if t >= slots:
                    dve.wait_ge(norms[name]["turned"], t + 1 - slots)

            dve.wait_ge(gain_in, 16)
            for t in range(TT + 1):
                if t < TT:
                    dve.wait_ge(norms["pre"]["rooted"], t + 1)
                    inverse(0, t)
                    slot_turned("pre", t)
                    dve.scalar_tensor_tensor(out=xn_first[:, t % 4, :], in0=x_tiles[:, t, :],
                                             scalar=stat[:, 0, 2, 0, t:t + 1], in1=gain[:, 0, :],
                                             op0=ALU.mult, op1=ALU.mult).then_inc(norms["pre"]["scaled"], 1)
                if t >= 2:
                    low_parts("pre", t - 1)
                if t == 0:
                    for n, (slot, src, _) in enumerate(first_units):
                        dve.wait_ge(first_high, n + 1)
                        dve.tensor_tensor(w_split[slot][:, 1, :], src, w_split[slot][:, 0, :].bitcast(fp32),
                                          ALU.subtract).then_inc(first_ready, 1)
                        if n == 0:
                            low_parts("pre", 0)

            dve.wait_ge(const_in, 16 * 3)
            for t in range(TT):
                dve.wait_ge(chunk_out, t + 1)
                groups = gv[:, t, :].rearrange("p (g c) -> p g c", g=GROUPS)
                gs = slice(t * GROUPS, (t + 1) * GROUPS)
                step(dve.tensor_reduce(g_sum[:, gs], groups, AX.X, ALU.add))
                step(dve.tensor_scalar(g_sum[:, gs], g_sum[:, gs], -1.0 / GROUP_DIM, None, ALU.mult))
                step(dve.tensor_tensor(groups, groups, g_sum[:, gs].unsqueeze(2).broadcast_to([P, GROUPS, GROUP_DIM]),
                                       ALU.add))
                sq = squares[:, t % 2, :]
                step(dve.tensor_tensor(sq, gv[:, t, :], gv[:, t, :], ALU.mult))
                ins = dve.tensor_reduce(g_var[:, gs], sq.rearrange("p (g c) -> p g c", g=GROUPS), AX.X, ALU.add)
                if t < TT - 1:
                    step(ins)
            ins.then_inc(var_ready, 1)
            dve.wait_ge(wf_in, 16)
            step(dve.tensor_copy(wf_split[:, 0, :, :], wf_raw[:, :, :]))
            dve.tensor_tensor(wf_split[:, 1, :, :], wf_raw[:, :, :], wf_split[:, 0, :, :].bitcast(fp32),
                              ALU.subtract).then_inc(wf_ready, 1)

            dve.wait_ge(var_rooted, 1)
            step(dve.reciprocal(g_inv[:, :], g_var[:, :]))
            for t in range(TT + 1):
                if t < TT:
                    groups = gv[:, t, :].rearrange("p (g c) -> p g c", g=GROUPS)
                    gs = slice(t * GROUPS, (t + 1) * GROUPS)
                    step(dve.tensor_tensor(groups, groups,
                                           g_inv[:, gs].unsqueeze(2).broadcast_to([P, GROUPS, GROUP_DIM]),
                                           ALU.mult))
                    dve.tensor_tensor(gv[:, t, :], gv[:, t, :], gain[:, 1, 0:D_GM], ALU.mult).then_inc(vn_scaled, 1)
                if t >= 1:
                    dve.wait_ge(vn_high, t)
                    dve.tensor_tensor(vn[:, 1, t - 1, :], gv[:, t - 1, :], vn[:, 0, t - 1, :].bitcast(fp32),
                                      ALU.subtract).then_inc(vn_ready, 1)

            z, ln1p, c_row = forget[0:HEADS, 0, :], forget[0:HEADS, 1, :], forget[0:HEADS, 2, :]
            dve.wait_ge(f_done, 1)
            dve.wait_ge(vn_ready, TT)
            dve.tensor_scalar(z.rearrange("p (b c) -> p b c", b=2), ps[0:HEADS, 0:2, :], bf_col[0:HEADS, 0:1], None,
                              ALU.add).then_inc(f_logit, 1)
            dve.wait_ge(f_logit, 1)

            for g in range(GROUPS):
                dve.wait_ge(spatial_done, g + 1)
                ch = slice(g * GROUP_DIM, (g + 1) * GROUP_DIM)
                dve.scalar_tensor_tensor(out=gu[:, :, ch], in0=ps[:, (g + 2) % 8, :].rearrange("p (n c) -> p n c", n=TT),
                                         scalar=bs_col[:, g:g + 1], in1=gu[:, :, ch],
                                         op0=ALU.add, op1=ALU.mult).then_inc(spatial_out, 1)

            dve.wait_ge(f_ln, 1)
            step(dve.scalar_tensor_tensor(out=ln1p, in0=z, scalar=0.0, in1=ln1p, op0=ALU.min, op1=ALU.subtract))
            step(dve.memset(z, 0.0))
            step(dve.tensor_tensor_scan(c_row, ln1p, z, 0.0, ALU.add, ALU.add))
            dve.tensor_scalar(c_row, c_row, -float(HEAD_DIM) ** 0.5, None, ALU.mult).then_inc(c_ready, 1)

            def score(turn_, j):
                a, q = TILES[j]
                n = (q + 1) * P
                if q == 0:
                    dve.wait_ge(bias_in[a], 16 * turn_ + 16)
                if at_ := lagged(turn_, j, 4):
                    dve.wait_ge(p_moved, N_PARTS * at_[0] + PART_AT[at_[1] + 1])
                dve.wait_ge(scores_done, N_TILES * turn_ + j + 1)
                dve.sem_inc(dve_passed, 1)
                src = ps[:, 2 * (j % 2):2 * (j % 2) + 2, :].rearrange("p b c -> p (b c)")[:, 0:n]
                dve.tensor_tensor_reduce(probs[:, j % 4, 0:n], src, forget_bias[:, a, 0:n],
                                         -float(HEAD_DIM) ** -0.5, 3e38, ALU.add, ALU.min,
                                         neg_max[:, j:j + 1]).then_inc(scored, 1)

            def probs_low(turn_, j):
                a, q = TILES[j]
                for part in range(PARTS[j]):
                    n = PART_AT[j] + part
                    dve.wait_ge(p_high, N_PARTS * turn_ + n + 1)
                    k0, k1 = 4 * part, min(q + 1, 4 * part + 4)
                    cols = slice(q % 2 * P, (q % 2 + 1) * P)
                    both = p_turned[j // 2 % 2]
                    dve.tensor_tensor(both[:, 1, k0:k1, cols],
                                      ps[:, 4 + n % 2, 0:(k1 - k0) * P].rearrange("p (k c) -> p k c", c=P),
                                      both[:, 0, k0:k1, cols].bitcast(fp32), ALU.subtract).then_inc(p_split, 1)

            def attend(turn_, m):
                a, blk = divmod(m, TT // 2)
                if m == 0:
                    dve.wait_ge(heads_ready, SPLITS * (2 * turn_ + 1) + 1)
                dve.wait_ge(exped, N_TILES * turn_ + 2 * m + 2)
                step(dve.reciprocal(row_inv[:, 2 * m:2 * m + 2], row_sum[:, 2 * m:2 * m + 2]))
                dve.wait_ge(folded, BLOCKS * turn_ + m + 1)
                for n in range(2):
                    t = 2 * blk + n
                    col = t * P + a * HEAD_DIM
                    ins = dve.tensor_scalar(qk_raw[:, bass.ds(turn_, 1), 0, col:col + HEAD_DIM].rearrange("p a n -> p (a n)"),
                                            ps[:, 7, n * HEAD_DIM:(n + 1) * HEAD_DIM],
                                            row_inv[:, 2 * m + n:2 * m + n + 1], None, ALU.mult)
                ins.then_inc(attended, 1)

            def mix_scaled(t):
                dve.wait_ge(norms["mix"]["rooted"], t + 1)
                dve.wait_ge(gain_in, 48)
                inverse(1, t, 2)
                slot_turned("mix", t)
                tok = slice(t * P, (t + 1) * P)
                for half, src in enumerate((qk_raw[:, :, 0, tok], gu[:, t, :])):
                    cols = slice(half * D_ATT, (half + 1) * D_ATT)
                    dst, g = xn_mix[:, t % 4, cols], gain[:, 0, cols]
                    if half == 0:
                        dst = dst.rearrange("p (a c) -> p a c", a=PAIRS)
                        g = g.rearrange("p (a c) -> p a c", a=PAIRS)
                    ins = dve.scalar_tensor_tensor(out=dst, in0=src, scalar=stat[:, 1, 2, half, t:t + 1],
                                                   in1=g, op0=ALU.mult, op1=ALU.mult)
                ins.then_inc(norms["mix"]["scaled"], 1)

            def dve_steps(turn_, steps):
                if not isinstance(turn_, int):
                    step.loop(turn_ - 1, BLOCKS)
                for j in range(steps):
                    if j < N_TILES:
                        score(turn_, j)
                    if at_ := lagged(turn_, j, 2):
                        probs_low(*at_)
                    if j == N_TILES + 2:
                        mix_scaled(0)
                        mix_scaled(1)
                    if (at_ := lagged(turn_, j, 4)) and at_[1] % 2 == 1:
                        attend(at_[0], at_[1] // 2)
                    if j == N_TILES + 3:
                        low_parts("mix", 0)
                if not isinstance(turn_, int):
                    step.end_loop(PAIRS - 2)

            for n in range(SPLITS):
                high, low, src, near = head_operand(0, 0, n)
                dve.wait_ge(heads_high, n + 1)
                dve.tensor_tensor(low, src, near.bitcast(fp32), ALU.subtract).then_inc(heads_ready, 1)
            pairs_of_heads(dve, dve_steps)
            dve.wait_ge(attended, BLOCKS * PAIRS)

            for t in range(2, TT + 1):
                if t < TT:
                    mix_scaled(t)
                low_parts("mix", t - 1)

            def post(norm, t, rooted, posted):
                dve.wait_ge(rooted, t + 1)
                inverse(norm, t)
                dve.scalar_tensor_tensor(out=y[:, t, :], in0=y[:, t, :], scalar=stat[:, norm, 2, 0, t:t + 1],
                                         in1=gain[:, 1, :], op0=ALU.mult, op1=ALU.mult).then_inc(posted, 1)

            for t in range(TT + 3):
                if t >= 3:
                    low_parts("ffn", t - 3)
                if t < TT:
                    post(2, t, post_rooted, h_posted)
                    if t >= TT - 2:
                        dve.wait_ge(h_posted, t + 1)
                        dve.wait_ge(h_in[t], 16)
                        dve.tensor_tensor(h[:, t, :], h[:, t, :], y[:, t, :], ALU.add).then_inc(h_late, 1)
                if 1 <= t <= TT:
                    n = t - 1
                    if t == 1:
                        dve.wait_ge(gain_in, 64)
                    dve.wait_ge(norms["ffn"]["rooted"], n + 1)
                    inverse(3, n)
                    slot_turned("ffn", n)
                    dve.scalar_tensor_tensor(out=xn_ffn[:, n % 4, :], in0=h[:, n, :], scalar=stat[:, 3, 2, 0, n:n + 1],
                                             in1=gain[:, 0, :], op0=ALU.mult, op1=ALU.mult
                                             ).then_inc(norms["ffn"]["scaled"], 1)

            for t in range(TT):
                dve.wait_ge(*h_signal(t))
                dve.memset(y[:, t, :], 0.0).then_inc(out_added, 1)

            def hidden(tile, unit):
                for half in range(2):
                    tile_full(dve, b_done, tile, unit, half)
                    dve.wait_ge(a_out, 2 * tile + half + 1)
                    dve.tensor_tensor(hid_raw[:, half, :], ps[:, 2 + half, :], silu_a[:, half, :],
                                      ALU.mult).then_inc(hid_made, 1)

            def hidden_low(slot, tile):
                for half in range(2):
                    cols = slice(half * BANK, (half + 1) * BANK)
                    dve.wait_ge(hid_high, 2 * tile + half + 1)
                    dve.tensor_tensor(hid[slot][:, 1, cols], hid_raw[:, half, :],
                                      hid[slot][:, 0, cols].bitcast(fp32), ALU.subtract).then_inc(hid_ready, 1)
                dve.wait_ge(hid_ready, 2 * tile + 2)

            def add_out(turn_, last_unit, t):
                for n in (2 * t, 2 * t + 1):
                    cols = slice(n % 2 * BANK, (n % 2 + 1) * BANK)
                    if n < 2 * TT - 1:
                        dve.wait_ge(out_done, (2 * TT - 1) * turn_ + n + 1)
                    else:
                        dve.wait_ge(w_used, last_unit + 1)
                    dve.tensor_tensor(y[:, t, cols], ps[:, 4 + n % 4, :], y[:, t, cols],
                                      ALU.add).then_inc(out_added, 1)

            for tile in range(2):
                hidden(tile, U_FFN + 2 * tile + 1)
                hidden_low(tile, tile)
            with dve.Fori(0, (FT // 2 - 1) // 2) as i:
                for g in range(2):
                    tile, unit = 4 * i + 2 * g + 2, U_FFN + 4 + 12 * i + 6 * g
                    hidden(tile, unit + 1)
                    dve.wait_ge(out_added, 32 * i + 16 * g + TT)
                    for t in range(TT):
                        add_out(2 * i + g, unit + 3, t)
                    hidden_low(0, tile)
                    hidden(tile + 1, unit + 5)
                    hidden_low(1, tile + 1)

            def embedding_out(t, bank):
                dve.wait_ge(e_squared, t + 1)
                dve.wait_ge(h2_ready, t + 1)
                dve.tensor_copy(y[:, t, :].rearrange("p (b c) -> p b c", b=2), ps[:, bank:bank + 2, :]
                                ).then_inc(e_out, 1)

            dve.wait_ge(out_added, 2 * TT * (FT // 2 - 1) + TT)
            dve.wait_ge(gain_in, 80)
            for t in range(TT + 1):
                if t < TT:
                    add_out(FT // 2 - 1, U_LAST + 1, t)
                if t >= 3:
                    low_parts("gate", t - 3, gate_bank(t - 3))
                if t < TT:
                    post(4, t, ffn_rooted, h2_posted)
                if t >= 2:
                    embedding_out(t - 2, 0 if t < TT else 4)
                if t < TT:
                    dve.wait_ge(pt_high, t + 1)
                    dve.tensor_tensor(pt_tile[t % 2][:, :, 1, :], pt_raw[:, :, t * P:(t + 1) * P],
                                      pt_tile[t % 2][:, :, 0, :].bitcast(fp32), ALU.subtract).then_inc(pt_ready, 1)
            embedding_out(TT - 1, 6)
            for t in range(TT - 2, TT):
                low_parts("gate", t, gate_bank(t))
            dve.wait_ge(norms["gate"]["rooted"], 1)
            dve.reciprocal(stat[:, 5, 2, 0, :], stat[:, 5, 1, 0, :]).then_inc(gate_inverted, 1)

            dve.wait_ge(gain_in, 96)
            dve.wait_ge(e_rooted, 1)
            step(dve.reciprocal(stat[:, 6, 2, 0, :], stat[:, 6, 1, 0, :]))
            for t in range(TT):
                dve.wait_ge(e_out, t + 1)
                dve.scalar_tensor_tensor(out=y[:, t, :], in0=y[:, t, :], scalar=stat[:, 6, 2, 0, t:t + 1],
                                         in1=gain[:, 0, :], op0=ALU.mult, op1=ALU.mult).then_inc(e_scaled, 1)
            for n in range(2 * TT):
                t, cols = n % TT, slice(n // TT * BANK, (n // TT + 1) * BANK)
                dve.wait_ge(e_scaled, t + 1)
                dve.wait_ge(gate_out, n + 1)
                step(dve.tensor_tensor(gates[:, n % 8, :], gates[:, n % 8, :], y[:, t, cols], ALU.mult))
                dve.tensor_tensor(h[:, t, cols], h[:, t, cols], gates[:, n % 8, :], ALU.add).then_inc(row_ready, 1)


def kernel(x, p, mix_pre_norm, mix_post_norm, w_in, b_forget, gm_v_norm, gm_w_s, gm_b_s, mix_out_norm,
           w_out, ffn_pre_norm, ffn_post_norm, w_ffn_in, w_ffn_out, w_ple, ple_norm, w_ple_gate):
    import concourse.bacc as bacc
    from concourse.bass_utils import run_bass_kernel_spmd

    f = lambda a: np.asarray(a)
    w_in, w_out, w_ffn_in, w_ffn_out, w_ple, w_gate = (
        f(a)[0] for a in (w_in, w_out, w_ffn_in, w_ffn_out, w_ple, w_ple_gate))

    def chunk(w):
        return w.reshape(-1, 2, P, BANK).transpose(0, 2, 1, 3).reshape(-1, P, UNIT)

    def columns(w):
        return w.reshape(1, KT, P, P).transpose(0, 2, 1, 3).reshape(1, P, UNIT)

    q0, k0, v0 = 0, D_ATT, 2 * D_ATT
    f0 = 3 * D_ATT
    g0 = f0 + HEADS
    units = [chunk(w_in[:, g0 + D_GM:]), chunk(w_in[:, g0:g0 + D_GM]), chunk(w_in[:, v0:v0 + D_ATT])]
    for pair in range(PAIRS):
        units += [columns(w_in[:, c + pair * P:c + (pair + 1) * P]) for c in (q0, k0)]
    units += [chunk(w_out[:, :BANK]), chunk(w_out[:, BANK:])]
    a = [columns(w_ffn_in[:, j * P:(j + 1) * P]) for j in range(FT)]
    b = [columns(w_ffn_in[:, D_FF + j * P:D_FF + (j + 1) * P]) for j in range(FT)]
    o = [w_ffn_out[None, j * P:(j + 1) * P, :] for j in range(FT)]
    for j in range(0, FT, 2):
        units += [a[j], b[j], *o[max(j - 2, 0):j], a[j + 1], b[j + 1]]
    units += [*o[FT - 2:], w_ple.reshape(2, P, UNIT), chunk(w_gate[:, :BANK]), chunk(w_gate[:, BANK:])]
    packed = np.concatenate(units, axis=0)
    assert packed.shape[0] == UNITS

    arrays = {
        "x": f(x)[0],
        "weights": packed,
        "w_forget": w_in[:, f0:g0].reshape(KT, P, HEADS).transpose(1, 0, 2),
        "b_forget": f(b_forget)[0][:, None],
        "p_t": f(p)[0, 0].T.reshape(2, P, TOKENS).transpose(1, 0, 2),
        "ws_t": f(gm_w_s)[0].transpose(2, 0, 1),
        "b_s": f(gm_b_s)[0].T,
        "gains": np.stack([f(g)[0] for g in (mix_pre_norm, mix_out_norm, mix_post_norm, ffn_pre_norm,
                                             ffn_post_norm, ple_norm)]),
        "gm_gain": f(gm_v_norm),
    }
    nc = bacc.Bacc("TRN2", target_bir_lowering=False, num_devices=1)
    fp32 = mybir.dt.float32
    aps = {}
    for name, value in arrays.items():
        arrays[name] = value = np.ascontiguousarray(value)
        aps[name] = nc.dram_tensor(name, value.shape, mybir.dt.from_np(value.dtype), kind="ExternalInput").ap()
    c_scratch = nc.dram_tensor("c_scratch", (HEADS, TOKENS), fp32).ap()
    out = nc.dram_tensor("out", (TOKENS, D_MODEL), fp32, kind="ExternalOutput").ap()
    build_trunk(nc, c_scratch=c_scratch, out=out, **aps)
    result = run_bass_kernel_spmd(nc, [arrays], core_ids=[0])
    return result.results[0]["out"].reshape(1, TOKENS, D_MODEL)
```
